# Optimizing a Trainium2 kernel written in Bass

```python
import math
import jax
import jax.numpy as jnp
from jax import lax
import numpy as np

D_MODEL = 2048
BATCH = 1
SEQ = 512
DEPTH = 1

F32 = jnp.float32
EPS = 1e-6
ATTN_HEADS = 6
ATTN_QK_DIM = 64
ATTN_V_DIM = 2 * ATTN_QK_DIM
ATTN_WIDTH = ATTN_HEADS * ATTN_V_DIM
Q_BLOCK = 128
REL_BUCKETS = 32
REL_MAX_DIST = 128
S5_GROUPS = 40
S5_GROUP_CH = 16
S5_STATE = 64
S5_WIDTH = S5_GROUPS * S5_GROUP_CH
HGRN_HEADS = 5
HGRN_DIM = 128
HGRN_WIDTH = HGRN_HEADS * HGRN_DIM
HGRN_CHUNK = 16
MIX_WIDTH = ATTN_WIDTH + S5_WIDTH + HGRN_WIDTH
SPLIT_SIZES = (ATTN_WIDTH, ATTN_WIDTH, ATTN_WIDTH, S5_WIDTH, HGRN_WIDTH, HGRN_WIDTH, HGRN_WIDTH, HGRN_WIDTH)
IN_COLS = 3 * ATTN_WIDTH + S5_WIDTH + 4 * HGRN_WIDTH
N_GROUPS = 4
EXPERTS_PER_GROUP = 8
N_EXPERTS = N_GROUPS * EXPERTS_PER_GROUP
TOP_K_IN_GROUP = 2
D_EXPERT = 512

kernel_name = 'hymba_style_diffattn_s5_hgrn2_hmoe'

def rms_norm(x, g):
    xf = x.astype(F32)
    y = xf * lax.rsqrt(jnp.mean(xf * xf, axis=-1, keepdims=True) + EPS)
    return (y * g.astype(F32)).astype(x.dtype)

def t5_bucket(dist):
    n = jnp.maximum(dist, 0)
    max_exact = REL_BUCKETS // 2
    large = max_exact + (jnp.log(jnp.maximum(n, 1).astype(F32) / max_exact)
                         / math.log(REL_MAX_DIST / max_exact) * (REL_BUCKETS - max_exact)).astype(jnp.int32)
    large = jnp.minimum(large, REL_BUCKETS - 1)
    return jnp.where(n < max_exact, n, large)

def diff_attention(q, k, v, rel_bias, lam_vecs, subln_g, layer_idx):
    B_, S_ = q.shape[0], q.shape[1]
    n_blocks = S_ // Q_BLOCK
    scale = ATTN_QK_DIM ** -0.5
    lam_init = 0.8 - 0.6 * math.exp(-0.3 * layer_idx)
    lv = lam_vecs.astype(F32)
    lam = jnp.exp(jnp.sum(lv[0] * lv[1])) - jnp.exp(jnp.sum(lv[2] * lv[3])) + lam_init
    qf = q.astype(F32).reshape(B_, n_blocks, Q_BLOCK, ATTN_HEADS, 2, ATTN_QK_DIM).transpose(1, 0, 2, 3, 4, 5)
    kf = k.astype(F32).reshape(B_, S_, ATTN_HEADS, 2, ATTN_QK_DIM)
    vf = v.astype(F32).reshape(B_, S_, ATTN_HEADS, ATTN_V_DIM)
    table = rel_bias.astype(F32)
    k_pos = jnp.arange(S_)

    def one_block(args):
        i, q_blk = args
        q_pos = i * Q_BLOCK + jnp.arange(Q_BLOCK)
        dist = q_pos[:, None] - k_pos[None, :]
        bias = jnp.transpose(table[t5_bucket(dist)], (2, 0, 1))
        logits = jnp.einsum('bqhmd,bkhmd->bhmqk', q_blk, kf) * scale + bias[None, :, None]
        logits = jnp.where((dist >= 0)[None, None, None], logits, -jnp.inf)
        p = jax.nn.softmax(logits, axis=-1)
        w = p[:, :, 0] - lam * p[:, :, 1]
        return jnp.einsum('bhqk,bkhv->bqhv', w, vf)

    out = lax.map(one_block, (jnp.arange(n_blocks), qf))
    out = out.transpose(1, 0, 2, 3, 4).reshape(B_, S_, ATTN_HEADS, ATTN_V_DIM)
    out = rms_norm(out, subln_g) * (1.0 - lam_init)
    return out.reshape(B_, S_, ATTN_WIDTH).astype(q.dtype)

def s5_mixer(u, a_re, a_im, log_dt, b_re, b_im, c_re, c_im, d_skip, w_glu):
    B_, S_ = u.shape[0], u.shape[1]
    uf = u.astype(F32).reshape(B_, S_, S5_GROUPS, S5_GROUP_CH)
    lr = jnp.minimum(a_re.astype(F32), -1e-4)
    li = a_im.astype(F32)
    dt = jnp.exp(log_dt.astype(F32))[:, None]
    mag = jnp.exp(lr * dt)
    ab_re = mag * jnp.cos(li * dt)
    ab_im = mag * jnp.sin(li * dt)
    den = lr * lr + li * li
    nr = ab_re - 1.0
    ni = ab_im
    f_re = (nr * lr + ni * li) / den
    f_im = (ni * lr - nr * li) / den
    br = b_re.astype(F32)
    bi = b_im.astype(F32)
    bb_re = f_re[..., None] * br - f_im[..., None] * bi
    bb_im = f_re[..., None] * bi + f_im[..., None] * br
    bu_re = jnp.einsum('bsgc,gnc->bsgn', uf, bb_re)
    bu_im = jnp.einsum('bsgc,gnc->bsgn', uf, bb_im)
    ar = jnp.broadcast_to(ab_re, bu_re.shape)
    ai = jnp.broadcast_to(ab_im, bu_re.shape)

    def combine(e1, e2):
        a1r, a1i, b1r, b1i = e1
        a2r, a2i, b2r, b2i = e2
        return (a1r * a2r - a1i * a2i, a1r * a2i + a1i * a2r,
                a2r * b1r - a2i * b1i + b2r, a2r * b1i + a2i * b1r + b2i)

    _, _, xr, xi = lax.associative_scan(combine, (ar, ai, bu_re, bu_im), axis=1)
    y = jnp.einsum('bsgn,gcn->bsgc', xr, c_re.astype(F32)) - jnp.einsum('bsgn,gcn->bsgc', xi, c_im.astype(F32))
    y = y + d_skip.astype(F32).reshape(S5_GROUPS, S5_GROUP_CH) * uf
    z = jax.nn.gelu(y.reshape(B_, S_, S5_WIDTH))
    out = z * jax.nn.sigmoid(jnp.einsum('bsc,ce->bse', z, w_glu.astype(F32)))
    return out.astype(u.dtype)

def hgrn2_mixer(q, f_logit, i_val, g, lb, norm_g):
    B_, S_ = q.shape[0], q.shape[1]
    N_ = S_ // HGRN_CHUNK
    shp = (B_, N_, HGRN_CHUNK, HGRN_HEADS, HGRN_DIM)
    lbf = lb.astype(F32)
    fl = f_logit.astype(F32)
    logf = jnp.logaddexp(jnp.log(lbf), jnp.log1p(-lbf) + jax.nn.log_sigmoid(fl)).reshape(shp)
    kf = ((1.0 - lbf) * jax.nn.sigmoid(-fl)).reshape(shp)
    qf = (jax.nn.silu(q.astype(F32)) * HGRN_DIM ** -0.5).reshape(shp)
    vf = i_val.astype(F32).reshape(shp)
    G = jnp.cumsum(logf, axis=2)
    causal = jnp.tril(jnp.ones((HGRN_CHUNK, HGRN_CHUNK), dtype=bool))
    diff = G[:, :, :, None] - G[:, :, None, :]
    decay = jnp.where(causal[None, None, :, :, None, None], jnp.exp(jnp.minimum(diff, 0.0)), 0.0)
    scores = jnp.einsum('bnthd,bnshd,bntshd->bnhts', qf, kf, decay)
    o_intra = jnp.einsum('bnhts,bnshv->bnthv', scores, vf)
    g_last = G[:, :, -1]
    k_dec = kf * jnp.exp(g_last[:, :, None] - G)
    U = jnp.einsum('bnshd,bnshv->bnhdv', k_dec, vf)
    chunk_decay = jnp.exp(g_last)

    def step(S, inp):
        dec, inc = inp
        return dec[..., None] * S + inc, S

    S0 = jnp.zeros((B_, HGRN_HEADS, HGRN_DIM, HGRN_DIM), F32)
    _, S_prev = lax.scan(step, S0, (jnp.moveaxis(chunk_decay, 1, 0), jnp.moveaxis(U, 1, 0)))
    o_inter = jnp.einsum('bnthd,nbhdv->bnthv', qf * jnp.exp(G), S_prev)
    o = (o_intra + o_inter).reshape(B_, S_, HGRN_HEADS, HGRN_DIM)
    o = rms_norm(o, norm_g) * jax.nn.sigmoid(g.astype(F32)).reshape(B_, S_, HGRN_HEADS, HGRN_DIM)
    return o.reshape(B_, S_, HGRN_WIDTH).astype(q.dtype)

def hier_moe(x, w_group, w_router, w_gate, w_up, w_down):
    B_, S_, D_ = x.shape
    xt = x.reshape(-1, D_)
    T_ = xt.shape[0]
    xr = xt.astype(F32)
    gl = jnp.einsum('td,dg->tg', xr, w_group.astype(F32))
    gp = jax.nn.softmax(gl, axis=-1)
    g_idx = jnp.argmax(gl, axis=-1)
    p_g = jnp.take_along_axis(gp, g_idx[:, None], axis=1)[:, 0]
    el = jnp.einsum('td,de->te', xr, w_router.astype(F32)).reshape(T_, N_GROUPS, EXPERTS_PER_GROUP)
    el_sel = jnp.take_along_axis(el, g_idx[:, None, None], axis=1)[:, 0]
    top_vals, top_idx = lax.top_k(el_sel, TOP_K_IN_GROUP)
    gates = jax.nn.softmax(top_vals, axis=-1) * p_g[:, None]
    expert_id = (g_idx[:, None] * EXPERTS_PER_GROUP + top_idx).reshape(-1)
    gates_flat = gates.reshape(-1)
    order = jnp.argsort(expert_id)
    token_of = order // TOP_K_IN_GROUP
    xs = xt[token_of]
    sizes = jnp.bincount(expert_id, length=N_EXPERTS).astype(jnp.int32)
    h = jax.nn.silu(lax.ragged_dot(xs, w_gate, sizes)) * lax.ragged_dot(xs, w_up, sizes)
    y = lax.ragged_dot(h, w_down, sizes)
    y = y * gates_flat[order][:, None].astype(y.dtype)
    out = jnp.zeros_like(xt).at[token_of].add(y)
    return out.reshape(B_, S_, D_)

def setup_inputs(seed: int = 0) -> dict:
    key = jax.random.key(seed)
    ks = jax.random.split(key, 26)

    def nrm(k, shape, scale):
        return jax.random.normal(k, shape, F32) * scale

    return {
        'x': nrm(ks[0], (BATCH, SEQ, D_MODEL), 1.0),
        'w_in': nrm(ks[1], (DEPTH, D_MODEL, IN_COLS), D_MODEL ** -0.5),
        'w_out': nrm(ks[2], (DEPTH, MIX_WIDTH, D_MODEL), MIX_WIDTH ** -0.5),
        'mix_norm_g': 1.0 + nrm(ks[3], (DEPTH, D_MODEL), 0.02),
        'ffn_norm_g': 1.0 + nrm(ks[4], (DEPTH, D_MODEL), 0.02),
        'rel_bias': nrm(ks[5], (REL_BUCKETS, ATTN_HEADS), 0.5),
        'diff_lambda': nrm(ks[6], (DEPTH, 4, ATTN_QK_DIM), 0.1),
        'attn_subln_g': 1.0 + nrm(ks[7], (DEPTH, ATTN_V_DIM), 0.02),
        's5_a_re': -0.5 + nrm(ks[8], (DEPTH, S5_GROUPS, S5_STATE), 0.01),
        's5_a_im': math.pi * jnp.arange(S5_STATE, dtype=F32) + nrm(ks[9], (DEPTH, S5_GROUPS, S5_STATE), 0.01),
        's5_log_dt': jax.random.uniform(ks[10], (DEPTH, S5_GROUPS), F32, math.log(1e-3), math.log(1e-1)),
        's5_b_re': nrm(ks[11], (DEPTH, S5_GROUPS, S5_STATE, S5_GROUP_CH), (2 * S5_GROUP_CH) ** -0.5),
        's5_b_im': nrm(ks[12], (DEPTH, S5_GROUPS, S5_STATE, S5_GROUP_CH), (2 * S5_GROUP_CH) ** -0.5),
        's5_c_re': nrm(ks[13], (DEPTH, S5_GROUPS, S5_GROUP_CH, S5_STATE), S5_STATE ** -0.5),
        's5_c_im': nrm(ks[14], (DEPTH, S5_GROUPS, S5_GROUP_CH, S5_STATE), S5_STATE ** -0.5),
        's5_d': nrm(ks[15], (DEPTH, S5_WIDTH), 1.0),
        's5_w_glu': nrm(ks[16], (DEPTH, S5_WIDTH, S5_WIDTH), S5_WIDTH ** -0.5),
        'hgrn_lb_logits': nrm(ks[17], (DEPTH, HGRN_WIDTH), 0.5),
        'hgrn_norm_g': 1.0 + nrm(ks[18], (DEPTH, HGRN_DIM), 0.02),
        'moe_w_group': nrm(ks[19], (DEPTH, D_MODEL, N_GROUPS), D_MODEL ** -0.5),
        'moe_w_router': nrm(ks[20], (DEPTH, D_MODEL, N_EXPERTS), D_MODEL ** -0.5),
        'moe_w_gate': nrm(ks[21], (DEPTH, N_EXPERTS, D_MODEL, D_EXPERT), D_MODEL ** -0.5),
        'moe_w_up': nrm(ks[22], (DEPTH, N_EXPERTS, D_MODEL, D_EXPERT), D_MODEL ** -0.5),
        'moe_w_down': nrm(ks[23], (DEPTH, N_EXPERTS, D_EXPERT, D_MODEL), D_EXPERT ** -0.5),
        'final_norm_g': 1.0 + nrm(ks[24], (D_MODEL,), 0.02),
    }

def reference(x, w_in, w_out, mix_norm_g, ffn_norm_g, rel_bias, diff_lambda, attn_subln_g,
              s5_a_re, s5_a_im, s5_log_dt, s5_b_re, s5_b_im, s5_c_re, s5_c_im, s5_d, s5_w_glu,
              hgrn_lb_logits, hgrn_norm_g, moe_w_group, moe_w_router, moe_w_gate, moe_w_up,
              moe_w_down, final_norm_g):
    lb_cum = jnp.cumsum(jax.nn.softmax(hgrn_lb_logits.astype(F32), axis=0), axis=0)
    lb_all = lb_cum - lb_cum[0:1]
    split_at = np.cumsum(SPLIT_SIZES)[:-1]
    h = x
    for l in range(DEPTH):
        xn = rms_norm(h, mix_norm_g[l])
        proj = jnp.einsum('bsd,de->bse', xn, w_in[l])
        q_a, k_a, v_a, u_s5, q_h, f_h, i_h, g_h = jnp.split(proj, split_at, axis=-1)
        attn_out = diff_attention(q_a, k_a, v_a, rel_bias, diff_lambda[l], attn_subln_g[l], l)
        s5_out = s5_mixer(u_s5, s5_a_re[l], s5_a_im[l], s5_log_dt[l], s5_b_re[l], s5_b_im[l],
                          s5_c_re[l], s5_c_im[l], s5_d[l], s5_w_glu[l])
        hgrn_out = hgrn2_mixer(q_h, f_h, i_h, g_h, lb_all[l], hgrn_norm_g[l])
        mix = jnp.concatenate([attn_out, s5_out, hgrn_out], axis=-1)
        h = h + jnp.einsum('bse,ed->bsd', mix, w_out[l]).astype(h.dtype)
        hn = rms_norm(h, ffn_norm_g[l])
        h = h + hier_moe(hn, moe_w_group[l], moe_w_router[l], moe_w_gate[l], moe_w_up[l], moe_w_down[l]).astype(h.dtype)
    return rms_norm(h, final_norm_g)


_drawn_inputs = setup_inputs


def setup_inputs(seed=0):
    import zlib

    import numpy as np

    out = dict(_drawn_inputs(seed))
    spreads = {}
    factors = {'attn_subln_g': 9.951,
     's5_a_re': 64.0,
     's5_log_dt': 21.528,
     's5_b_re': 23.264,
     's5_b_im': 23.952,
     's5_c_re': 25.656,
     's5_c_im': 22.008,
     'hgrn_norm_g': 13.382,
     'final_norm_g': 8.126,
     'ffn_norm_g': 3.732,
     's5_a_im': 8.0}
    for name, (base, spread) in spreads.items():
        noise = np.random.default_rng([zlib.crc32(name.encode()), seed]).standard_normal(out[name].shape)
        drawn = base * np.exp(spread * noise) if base else spread * noise
        out[name] = jnp.asarray(drawn.astype(out[name].dtype))
    for name, factor in factors.items():
        out[name] = (out[name] * factor).astype(out[name].dtype)
    return out
```

```python
import math
from contextlib import ExitStack

import numpy as np

import concourse.bass as bass
from concourse import mybir

ALU = mybir.AluOpType
ACT = mybir.ActivationFunctionType
AX = mybir.AxisListType
F32 = mybir.dt.float32
U32 = mybir.dt.uint32
I32 = mybir.dt.int32

P = 128
EPS = 1e-6
D = 2048
S = 512
TB = S // P
KD = D // P
AH, QK, AV = 6, 64, 128
SG, SC, SN = 40, 16, 64
HH, HD = 5, 128
LC = 8
NC5 = S // LC
NB5 = SG // 8
QB = 4
NQ = SG // 2
NE, EPG, NGRP, FE = 32, 8, 4, 512
CAP = 96
NOV = 2 * S // CAP
NT = NE + NOV
SENT = 4096.0
BIG = 1.0e30
LAM_INIT = 0.8 - 0.6 * math.exp(-0.3 * 0)
RB = 640
LEVELS = [1, 2, 4, 8, 16, 32, 64]
NIN = 5504
COLS = {"qa": 0, "ka": 768, "va": 1536, "u": 2304, "qh": 2944, "fh": 3584, "ih": 4224, "gh": 4864}


def shape_constants():
    i = np.arange(P)
    s, t = i[:, None], i[None, :]
    parts = {
        "ident": (s == t),
        "tri": (s < t),
        "ones": np.ones((P, P)),
    }
    for L in LEVELS:
        parts[f"mask{L}"] = (s // (2 * L) == t // (2 * L)) & (s % (2 * L) < L) & (t % (2 * L) >= L)
    parts["rev"] = np.broadcast_to(NE - np.arange(NE), (P, NE))
    parts["base"] = np.broadcast_to(CAP * np.arange(NE), (P, NE))
    parts["over"] = np.broadcast_to(CAP * (NE - 1 - np.arange(NE)), (P, NE))
    parts["ovi"] = np.broadcast_to(np.arange(NOV), (P, NOV))
    parts["tok"] = i[:, None] + P * np.arange(TB)[None, :]
    cols, at = {}, 0
    for k, v in parts.items():
        cols[k] = (at, v.shape[1])
        at += v.shape[1]
    block = np.concatenate([np.asarray(v, np.float32) for v in parts.values()], axis=1)
    dist = S - 1 - np.arange(RB)
    n = np.maximum(dist, 0)
    large = 16 + (np.log(np.maximum(n, 1).astype(np.float32) / 16) / math.log(128 / 16) * 16).astype(np.int32)
    bucket = np.where(n < 16, n, np.minimum(large, 31))
    onehot = (bucket[None, :] == np.arange(32)[:, None]).astype(np.float32)
    masked = np.broadcast_to(np.where(dist >= 0, 0.0, -BIG).astype(np.float32), (AH, RB))
    return np.ascontiguousarray(block), cols, np.ascontiguousarray(onehot), np.ascontiguousarray(masked)


def build(nc, d, out, cc):
    ctx = ExitStack()
    with ctx:
        def sem(name):
            return ctx.enter_context(nc.semaphore(name))

        W = 53100
        arena = ctx.enter_context(nc.sbuf_tensor("arena", [P, W], F32))
        abase = arena[:, :]
        psum = ctx.enter_context(nc.psum_tensor("psum", [P, 8 * 512], F32))
        pbase = psum[:, :]

        def V(off, dims, p0=0, n=P):
            return bass.AP(tensor=abase.tensor, offset=p0 * W + off, ap=[[W, n]] + [[s, c] for s, c in dims])

        def F(off, n, p0=0, parts=P):
            return V(off, [(1, n)], p0, parts)

        def B(bank, dims, p0=0, n=P, off=0):
            return bass.AP(tensor=pbase.tensor, offset=p0 * 4096 + bank * 512 + off,
                           ap=[[4096, n]] + [[s, c] for s, c in dims])

        def DV(t, off, dims):
            return bass.AP(tensor=t.tensor, offset=t.offset + off, ap=[[s, c] for s, c in dims])

        at = [0]

        def take(n):
            at[0] += n
            return at[0] - n

        ncon = sum(n for _, n in cc.values())
        CON = take(ncon)
        C = {k: CON + o for k, (o, _) in cc.items()}
        IDENT = C["ident"]
        WR = take(KD * 36)
        GMIX = take(KD)
        LBL, LBE, LBR, LB, LB1, D5 = take(HH), take(HH), take(HH), take(HH), take(HH), take(NB5)
        SUB, SUBG, HNG = take(1), take(1), take(1)
        LAMD, LAME, NLAM = take(2), take(2), take(1)
        FRI = take(2 * NQ)
        SSQ, STD, RST, EPSC = take(TB), take(TB), take(TB), take(1)
        SM = take(24)
        R0 = take(TB * 2)
        HST = take(2 * TB)
        TOT = take(HH * TB)
        GATE = take(2 * TB)
        SLOTF, TOKU, DSTU = take(NT + 1), take(NT + 1), take(NT + 1)
        EID = take(NOV + 1)
        LDT = take(2)
        GIDX, SIDX = take(1), take(1)
        H0 = 2600
        assert at[0] <= H0, at[0]
        A0 = H0 + 8192
        X0 = A0 + 16384
        M0 = X0 + 8192
        E0 = M0 + 8192
        NW, WS = 3, 2048
        RING = [E0 + i * WS for i in range(NW)]
        W1T = E0 + NW * WS
        KBUF = W1T + 1024
        PT = KBUF + 1024
        assert PT + 1152 <= W
        CNAT, OH, RM, RR, LAML, RELB, BRAW, CRI = (A0, A0 + 1280, A0 + 1920, A0 + 2560, A0 + 3200, A0 + 3456,
                                                   A0 + 3600, A0 + 4480)
        LAMP = A0 + 4240
        VH, GH = A0, A0 + 2560
        UT, ZT = A0 + 5120, A0 + 7680
        S5T = A0 + 10240
        CA = S5T + 1024
        SX = CA + 1152
        ST = SX + 512
        W1 = ST + 1024
        YP = W1 + 1024
        assert YP + 512 <= X0
        PW = M0
        PR = PW + 540
        SP = PR + 320
        BB = SP + 240
        UP, YT = M0 + 2048, M0 + 2560
        assert BB + 640 <= UP
        DS = M0 + 11 * 512
        MS5 = M0 + 6 * 512
        FT, KT, QT, HO = H0, H0 + 2560, H0 + 5120, H0 + 7680
        AQ, AK = A0 + 5120, A0 + 8192
        HAT = A0 + 11264
        HT2 = HAT + 2560
        STRIP = HT2 + 1280
        assert STRIP + 1024 <= X0
        HS, HKN, HSQ = FT, HT2, HT2 + 768
        AVV = A0
        AL = [HAT, A0 + 3072]
        AW = [HAT + 1024, HAT + 1536]
        AWT = [HAT + 2048, HT2]
        AO, ASQ = A0 + 4096, A0 + 4608
        GF, HSB, JUNK = E0, E0 + 2048, E0 + 6144
        at[0] = E0 + 6144
        RLG, RGM, RGD, RGE, ROG, RTMP, RCM, REL = (take(n) for n in (144, 4, 16, 16, 16, 128, 4, 128))
        RV1, RV2, RO1, RO2, RDF, RE2, AS, RGS = (take(n) for n in (4, 4, 128, 128, 4, 4, 128, 4))
        RCN, RNV, RCU, ROB, RPF, IDS, POSU, RBG, REI, LSI = (
            take(n) for n in (NE, NE, NE, NE, 8, 8, 8, NE * NOV, NOV + 1, CAP))
        assert at[0] <= W
        EIDV = F(EID, NOV + 1, 0, 1).bitcast(I32)
        TOKV, DSTV = F(TOKU, NT + 1).bitcast(U32), F(DSTU, NT + 1).bitcast(U32)

        def scratch(name, shape):
            return nc.dram_tensor(name, shape, F32, kind="Internal").ap()

        u_d = scratch("u_scratch", [NB5 * P, S])
        y_d = scratch("y_scratch", [NB5 * P, S])
        r_d = scratch("bias_rows", [AH * P, RB])
        hs_d = scratch("hs_rows", [S, D])
        ex_d = scratch("expert_rows", [2 * S, D])
        list_d = scratch("slot_list", [NT * CAP, 1])

        def project(kind, n):
            return [("pj", kind, j) for j in range(n)]

        steps = [("xT", t, q) for t in range(TB) for q in range(4)]
        steps += project("u", 5)
        steps += [("ab",), ("cT", 0), ("cT", 1), ("cT", 2), ("rb", 0), ("rb", 1)]
        s5 = []
        for b in range(NB5):
            s5 += [[("w1T", b, 0), ("w1T", b, 1), ("kk", b, 0), ("kk", b, 1), ("st", b)], [], [("y5", b, 0), ("y5", b, 1)]]
        mid = project("fh", 5) + project("qh", 5) + project("ih", 5) + project("gh", 5)
        GELU_AFTER = {mid[3 * b + 4][1:]: b for b in range(NB5)}
        for j, m in enumerate(mid):
            steps.append(m)
            if 1 <= j <= 15:
                steps += s5[j - 1]
        steps += project("glu", 5)
        hg = [[("hs", l, h) for h in range(HH)] for l in range(8)]
        hg += [[("hk", 0), ("hk", 1), ("hu", 0), ("hk", 2), ("hu", 1), ("hk", 3), ("hu", 2), ("hk", 4), ("hu", 3),
                ("hu", 4)],
               [("ho", 0), ("ho", 1), ("ho", 2)], [("ho", 3), ("ho", 4), ("hz", 0), ("hz", 1)],
               [("hz", 2), ("hz", 3), ("hz", 4)]]
        for j, m in enumerate(project("qa", 6) + project("ka", 6)):
            steps.append(m)
            steps += hg[j]
        steps += project("va", 6)
        units = [(h, i) for h in range(AH) for i in range(TB)]
        for n in range(len(units) + 2):
            if n < len(units):
                steps += [("al",) + units[n] + (0,), ("al",) + units[n] + (1,)]
            if 1 <= n <= len(units):
                steps.append(("aw",) + units[n - 1])
            if n >= 2:
                h, i = units[n - 2]
                steps.append(("ao", h, i))
                if i == 1 and h >= 1:
                    steps.append(("az", h - 1))
        steps.append(("az", AH - 1))
        steps += project("wo", 16)
        steps += [("hT", t, q) for t in range(TB) for q in range(4)]
        steps += [("rt",), ("rk",), ("id",)]
        chunks = [s[1:] for s in steps if s[0] == "pj"]
        chunk_no = {c: i for i, c in enumerate(chunks)}
        use, turn, uses = {}, 0, [0] * 8
        for s in steps:
            if s[0] == "ao":
                use[s] = (7, s[1])
                continue
            use[s] = (turn % 7, uses[turn % 7])
            uses[turn % 7] += 1
            turn += 1
        uses[7] = AH

        full = [sem(f"bank_full{i}") for i in range(8)]
        free = [sem(f"bank_free{i}") for i in range(8)]
        dve_step, pool_step, pool_passed = sem("dve_step"), sem("pool_step"), sem("pool_passed")
        chunk_in = [sem(f"chunk_in{i}") for i in range(NW)]
        consts_in, params_in, disc_in, cnat_in = sem("consts_in"), sem("params_in"), sem("disc_in"), sem("cnat_in")
        strip_in = [sem("strip_in0"), sem("strip_in1")]
        x_in = [sem(f"x_in{i}") for i in range(TB)]
        x_std, x_scaled = sem("x_std"), sem("x_scaled")
        disc_act, disc_dve, disc_done = sem("disc_act"), sem("disc_dve"), sem("disc_done")
        tables_ready = sem("tables_ready")
        lb_dve, lb_act, lam_dve, lam_act = sem("lb_dve"), sem("lb_act"), sem("lam_dve"), sem("lam_act")
        w1_ready, ca_ready, t_zero, t_ready = sem("w1_ready"), sem("ca_ready"), sem("t_zero"), sem("t_ready")
        up_in, u_out = sem("up_in"), [sem(f"u_out{b}") for b in range(NB5)]
        scanned, y_out, yT_in, yT_sum = sem("scanned"), sem("y_out"), sem("yT_in"), sem("yT_sum")
        z_ready, s5_mixed = sem("z_ready"), sem("s5_mixed")
        level_ready, ho_std, ho_ready = sem("level_ready"), sem("ho_std"), sem("ho_ready")
        bias_row, bias_out, strip_used = sem("bias_row"), sem("bias_out"), sem("strip_used")
        act_step, eps_set, ao_std = sem("act_step"), sem("eps_set"), sem("ao_std")
        l_ready, e_ready, w_ready, ao_ready = sem("l_ready"), sem("e_ready"), sem("w_ready"), sem("ao_ready")
        x_again, h_std, gf_in, hs_ready = sem("x_again"), sem("h_std"), sem("gf_in"), sem("hs_ready")
        hs_out = [sem("hs_out0"), sem("hs_out1")]
        groups_diff, groups_exp, gates_diff, gates_exp = (
            sem("groups_diff"), sem("groups_exp"), sem("gates_diff"), sem("gates_exp"))
        onehots_ready, list_clear, list_init = sem("onehots_ready"), sem("list_clear"), sem("list_init")
        pos_ready, list_out, list_in, slots_ready = (
            sem("pos_ready"), sem("list_out"), sem("list_in"), sem("slots_ready"))
        slot_in = [sem(f"slot_in{i}") for i in range(8)]
        slot_used = [sem(f"slot_used{i}") for i in range(8)]
        gidx_set, sidx_set, rows_in, rows_out = sem("gidx_set"), sem("sidx_set"), sem("rows_in"), sem("rows_out")
        ysb_free = sem("ysb_free")
        xg_clear, xT_full, xT_free = sem("xg_clear"), sem("xT_full"), sem("xT_free")
        silu_done, h_done, y_full, y_act, y_dve = (
            sem("silu_done"), sem("h_done"), sem("y_full"), sem("y_act"), sem("y_dve"))
        moe_done, fin_in, fg_in = sem("moe_done"), [sem(f"fin_in{i}") for i in range(TB)], sem("fg_in")
        sum_ready, sum_std, out_ready, out_done = (
            sem("sum_ready"), sem("sum_std"), sem("out_ready"), sem("out_done"))

        def take_bank(pe, s):
            bank, n = use[s]
            if n:
                pe.wait_ge(free[bank], n)
            return bank

        def see_bank(eng, s):
            bank, n = use[s]
            eng.wait_ge(full[bank], n + 1)
            return bank

        def see_copy(eng, s):
            bank, n = use[s]
            eng.wait_ge(free[bank], n + 1)

        SLOT = [A0 + i * 4096 for i in range(8)]
        XG, YSB, XT, HTE, SIL = E0, E0 + 2048, [E0 + 4096, E0 + 4096 + KD * CAP], E0 + 4096 + 2 * KD * CAP, \
            E0 + 4096 + 2 * KD * CAP + 4 * CAP
        assert SIL + 4 * CAP <= W
        FT2 = FE // P

        def main_part(it, k, j):
            L = 6 * k + j
            return L % 8, it * 3 + L // 8

        def over_part(it, k, j):
            return j, 24 + it * 2 + k

        wg_d, wu_d, wd_d = d["moe_w_gate"], d["moe_w_up"], d["moe_w_down"]

        block = ctx.enter_context(nc.Block())

        @block.sync
        def _(sp):
            for t in range(TB):
                sp.dma_start(F(H0 + t * D, D), DV(d["x"], t * P * D, [(D, P), (1, D)])).then_inc(x_in[t], 16)

            def chunk(i):
                kind, j = chunks[i]
                if i >= NW:
                    see_bank(sp, ("pj",) + chunks[i - NW])
                if kind == "glu":
                    rows, src = 5, DV(d["s5_w_glu"], j * P, [(640, P), (P * 640, 5), (1, P)])
                elif kind == "wo":
                    rows, src = KD, DV(d["w_out"], j * P, [(D, P), (P * D, KD), (1, P)])
                else:
                    rows, src = KD, DV(d["w_in"], COLS[kind] + j * P, [(KD * NIN, P), (NIN, KD), (1, P)])
                sp.dma_start(V(RING[i % NW], [(P, rows), (1, P)]), src).then_inc(chunk_in[i % NW], 16)

            for i in range(len(chunks)):
                if chunks[i] == ("wo", 0):
                    see_copy(sp, ("hz", HH - 1))
                    for t in range(TB):
                        sp.dma_start(F(H0 + t * D, D),
                                     DV(d["x"], t * P * D, [(D, P), (1, D)])).then_inc(x_again, 16)
                chunk(i)
            for c in chunks[-NW:]:
                see_bank(sp, ("pj",) + c)
            sp.dma_start(F(GF, D), DV(d["ffn_norm_g"], 0, [(0, P), (1, D)])).then_inc(gf_in, 16)
            for t in range(TB):
                sp.wait_ge(hs_ready, t + 1)
                sp.dma_start(DV(hs_d, t * P * D, [(D, P), (1, D)]), F(HSB + (t % 2) * D, D)).then_inc(hs_out[t % 2], 16)

            def part(e, place, j):
                slot, n = place
                sp.wait_ge(slot_used[slot], n + 1)
                if j < 4:
                    w = wg_d if j < 2 else wu_d
                    src = w[bass.ds(e, 1), :, :].rearrange("e (p c) n -> p (e c n)", p=P)[:, (j % 2) * 4096:
                                                                                         (j % 2 + 1) * 4096]
                    dst = F(SLOT[slot], 4096)
                else:
                    src = wd_d[bass.ds(e, 1), (j - 4) * 256:(j - 3) * 256, :].rearrange("e (m p) n -> p (e m) n", p=P)
                    dst = V(SLOT[slot], [(D, 2), (1, D)])
                sp.dma_start(dst, src).then_inc(slot_in[slot], 16)

            see_copy(sp, ("az", AH - 1))
            see_bank(sp, ("rt",))
            with sp.Fori(0, NE // 4) as it:
                for k in range(4):
                    for j in range(6):
                        part(it * 4 + k, main_part(it, k, j), j)
            sp.wait_ge(slots_ready, 1)
            flag = sp.value_load(F(EID + NOV, 1, 0, 1).bitcast(I32), min_val=0, max_val=NOV)
            with sp.If(flag > 0):
                with sp.Fori(0, NOV // 2) as it:
                    for k in range(2):
                        e = sp.value_load(EIDV[0:1, bass.ds(it * 2 + k, 1)], min_val=0, max_val=NE - 1)
                        for j in range(6):
                            part(e, over_part(it, k, j), j)
            sp.wait_ge(moe_done, 1)
            sp.dma_start(F(A0, D), DV(d["final_norm_g"], 0, [(0, P), (1, D)])).then_inc(fg_in, 16)
            for t in range(TB):
                for k in range(2):
                    sp.dma_start(F(A0 + D * (1 + 2 * t + k), D),
                                 DV(ex_d, (k * S + t * P) * D, [(D, P), (1, D)])).then_inc(fin_in[t], 16)
            for t in range(TB):
                sp.wait_ge(out_ready, t + 1)
                sp.dma_start(DV(out, t * P * D, [(D, P), (1, D)]), F(A0 + D * (1 + 2 * t), D)).then_inc(out_done, 16)
            sp.wait_ge(out_done, 16 * TB)

        @block.gpsimd
        def _(pool):
            g = nc.gpsimd
            for s in slot_used + [silu_done, h_done, y_act, y_dve, ysb_free]:
                pool.sem_inc(s, 1)
            steps_p = [0]

            def settle(ins):
                steps_p[0] += 1
                ins.then_inc(pool_step, 1)
                pool.wait_ge(pool_step, steps_p[0])

            for dst, src in [
                (F(CON, ncon), d["consts"]),
                (F(GMIX, KD), DV(d["mix_norm_g"], 0, [(KD, P), (1, KD)])),
            ]:
                pool.dma_start(dst, src, allow_slow_non_contiguous=True).then_inc(consts_in, 16)
            for dst, src in [
                (F(DS, P, 0, NQ), DV(d["s5_a_re"], 0, [(P, NQ), (1, P)])),
                (F(DS + P, P, 0, NQ), DV(d["s5_a_im"], 0, [(P, NQ), (1, P)])),
                (F(LDT, 2, 0, NQ), DV(d["s5_log_dt"], 0, [(2, NQ), (1, 2)])),
            ]:
                pool.dma_start(dst, src, allow_slow_non_contiguous=True).then_inc(disc_in, 16)
            for i, name in enumerate(("s5_c_re", "s5_c_im")):
                for half in range(2):
                    pool.dma_start(V(CNAT + i * 640 + half * SN, [(P, 5), (1, SN)]),
                                   DV(d[name], 0, [(SN, P), (P * SN, 5), (1, SN)])).then_inc(cnat_in, 16)
            for dst, src in [
                (V(BRAW, [(SC, NQ), (1, SC)]), DV(d["s5_b_re"], 0, [(SC, P), (P * SC, NQ), (1, SC)])),
                (V(BRAW + 320, [(SC, NQ), (1, SC)]), DV(d["s5_b_im"], 0, [(SC, P), (P * SC, NQ), (1, SC)])),
                (V(WR, [(36, KD), (1, 4)]), DV(d["moe_w_group"], 0, [(KD * 4, P), (4, KD), (1, 4)])),
                (V(WR + 4, [(36, KD), (1, 32)]), DV(d["moe_w_router"], 0, [(KD * 32, P), (32, KD), (1, 32)])),
                (F(LBL, HH), DV(d["hgrn_lb_logits"], 0, [(1, P), (P, HH)])),
                (F(D5, NB5), DV(d["s5_d"], 0, [(1, P), (P, NB5)])),
                (F(SUB, 1), DV(d["attn_subln_g"], 0, [(1, P), (1, 1)])),
                (F(HNG, 1), DV(d["hgrn_norm_g"], 0, [(1, P), (1, 1)])),
                (F(LAML, 256), DV(d["diff_lambda"], 0, [(0, P), (1, 256)])),
                (F(OH, RB, 0, 32), d["onehot"]),
                (F(RM, RB, 0, AH), d["masked"]),
                (F(RELB, AH, 0, 32), DV(d["rel_bias"], 0, [(AH, 32), (1, AH)])),
            ]:
                pool.dma_start(dst, src, allow_slow_non_contiguous=True).then_inc(params_in, 16)
            g.memset(F(S5T, 1024), 0.0).then_inc(t_zero, 1)
            pool.wait_ge(bias_row, 1)
            pool.dma_start(DV(r_d, 0, [(P * RB, AH), (RB, P), (1, RB)]),
                           V(RR, [(0, P), (1, RB)], 0, AH)).then_inc(bias_out, 16)

            def w1(b):
                for ri in range(2):
                    br, bi = (0, 1) if ri == 0 else (1, 0)
                    pw = [V(PR + x * 160 + QB * b, [(1, QB), (NQ, LC), (0, SC)]) for x in range(2)]
                    bb = [V(BB + x * 320 + QB * b * SC, [(SC, QB), (0, LC), (1, SC)]) for x in (br, bi)]
                    prod = [V(PT + x * 576, [(P, QB), (SC, LC), (1, SC)]) for x in range(2)]
                    g.tensor_tensor(prod[0], pw[0], bb[0], ALU.mult)
                    settle(g.tensor_tensor(prod[1], pw[1], bb[1], ALU.mult))
                    g.tensor_tensor(F(W1 + ri * 512, 512), F(PT, 512), F(PT + 576, 512),
                                    ALU.subtract if ri == 0 else ALU.add).then_inc(w1_ready, 1)
                    pool.wait_ge(w1_ready, 2 * b + ri + 1)

            def ca(b):
                for ri in range(2):
                    pw = [V(PW + x * 180 + QB * b, [(1, QB), (NQ, 9), (0, SC)]) for x in ((0, 1) if ri == 0 else (2, 0))]
                    cc_ = [V(CRI + x * 320 + QB * b * SC, [(SC, QB), (0, 9), (1, SC)]) for x in range(2)]
                    prod = [V(PT + x * 576, [(144, QB), (SC, 9), (1, SC)]) for x in range(2)]
                    g.tensor_tensor(prod[0], cc_[0], pw[0], ALU.mult)
                    settle(g.tensor_tensor(prod[1], cc_[1], pw[1], ALU.mult))
                    g.tensor_tensor(F(CA + ri * 576, 576), F(PT, 576), F(PT + 576, 576),
                                    ALU.subtract).then_inc(ca_ready, 1)
                    pool.wait_ge(ca_ready, 2 * b + ri + 1)

            pool.wait_ge(tables_ready, 1)
            w1(0)
            ca(0)
            for b in range(NB5):
                see_copy(pool, ("pj", "u", b))
                pool.dma_start(DV(u_d, b * P * S, [(S, P), (1, S)]), F(UT + b * S, S)).then_inc(u_out[b], 16)
            for b in range(NB5):
                pool.wait_ge(u_out[b], 16)
                if b >= 1:
                    see_bank(pool, ("y5", b - 1, 1))
                for j in range(LC):
                    pool.dma_start(V(UP, [(NC5, 8), (1, NC5)], SC * j, SC),
                                   DV(u_d, b * P * S + j * NC5, [(S, SC), (SC * S, 8), (1, NC5)])).then_inc(up_in, 16)
                for half in range(2):
                    see_copy(pool, ("kk", b, half))
                for j in range(LC):
                    n = P - SC * j
                    pool.dma_start(V(S5T + SC * j, [(P, 8), (1, n)], SC * j, SC),
                                   V(KBUF, [(P, 8), (1, n)], 0, SC)).then_inc(t_ready, 16)
                if b + 1 < NB5:
                    for ri in range(2):
                        see_bank(pool, ("w1T", b, ri))
                    w1(b + 1)
                for par in range(2):
                    see_copy(pool, ("y5", b, par))
                for j in range(LC):
                    pool.dma_start(DV(y_d, b * P * S + j * NC5, [(S, SC), (SC * S, 8), (1, NC5)]),
                                   V(YP, [(NC5, 8), (1, NC5)], SC * j, SC)).then_inc(y_out, 16)
                if b + 1 < NB5:
                    ca(b + 1)
                pool.wait_ge(y_out, 16 * LC * (b + 1))
                if b >= 1:
                    pool.wait_ge(z_ready, b)
                pool.dma_start(F(YT, S), DV(y_d, b * P * S, [(S, P), (1, S)])).then_inc(yT_in, 16)

            pool.wait_ge(bias_out, 16)
            for h in range(AH):
                if h >= 2:
                    pool.wait_ge(strip_used, h - 1)
                pool.dma_start(F(STRIP + (h % 2) * 512, 512),
                               DV(r_d, h * P * RB + P - 1, [(RB - 1, P), (1, 512)])).then_inc(strip_in[h % 2], 16)

            pool.wait_ge(list_clear, 1)
            pool.dma_start(list_d.rearrange("(n s) o -> n (s o)", s=CAP), F(LSI, CAP, 0, NT)).then_inc(list_init, 16)
            pool.wait_ge(list_init, 16)
            pool.wait_ge(pos_ready, 1)
            for k in range(2 * TB):
                g.indirect_dma_start(out=list_d[:, :], out_offset=bass.IndirectOffsetOnAxis(
                    ap=F(POSU + k, 1).bitcast(U32), axis=0), in_=F(IDS + k, 1), in_offset=None,
                    bounds_check=NT * CAP - 1, oob_is_err=False).then_inc(list_out, 16)
            pool.wait_ge(list_out, 16 * 2 * TB)
            pool.dma_start(F(LSI, CAP, 0, NT), list_d.rearrange("(n s) o -> n (s o)", s=CAP)).then_inc(list_in, 16)
            g.memset(F(XG, D, 0, CAP), 0.0).then_inc(xg_clear, 1)
            pool.wait_ge(xg_clear, 1)
            pool.wait_ge(slots_ready, 1)
            for s in hs_out:
                pool.wait_ge(s, 32)
            sent = [0]

            def gather(n):
                g.tensor_copy(F(GIDX, 1, 0, CAP).bitcast(U32), TOKV[0:CAP, bass.ds(n, 1)]).then_inc(gidx_set, 1)
                pool.wait_ge(gidx_set, n + 1)
                pool.sem_inc(pool_passed, 1)
                g.indirect_dma_start(out=F(XG, D, 0, CAP), out_offset=None, in_=hs_d[:, :],
                                     in_offset=bass.IndirectOffsetOnAxis(ap=F(GIDX, 1, 0, CAP).bitcast(U32), axis=0),
                                     bounds_check=S - 1, oob_is_err=False).then_inc(rows_in, 16)

            def tile(n):
                pool.wait_ge(xT_full, 4 * n + 4)
                gather(n + 1)
                g.tensor_copy(F(SIDX, 1, 0, CAP).bitcast(U32), DSTV[0:CAP, bass.ds(n, 1)]).then_inc(sidx_set, 1)
                pool.wait_ge(sidx_set, n + 1)
                pool.wait_ge(y_act, 2 * n + 3)
                pool.wait_ge(y_dve, 2 * n + 3)
                pool.sem_inc(pool_passed, 1)
                g.indirect_dma_start(out=ex_d[:, :], out_offset=bass.IndirectOffsetOnAxis(
                    ap=F(SIDX, 1, 0, CAP).bitcast(U32), axis=0), in_=F(YSB, D, 0, CAP), in_offset=None,
                    bounds_check=2 * S - 1, oob_is_err=False).then_inc(rows_out, 16)
                pool.wait_ge(rows_out, 16 * n + 16)
                pool.sem_inc(ysb_free, 1)

            gather(0)
            with pool.Fori(0, NE // 2) as it:
                for k in range(2):
                    tile(it * 2 + k)
            flag = pool.value_load(F(EID + NOV, 1, 0, 1).bitcast(I32), min_val=0, max_val=NOV)
            with pool.If(flag > 0):
                with pool.Fori(0, NOV // 2) as it:
                    for k in range(2):
                        tile(it * 2 + k + NE)
            pool.sem_inc(moe_done, 1)

        @block.tensor
        def _(pe):
            mm, tr = nc.tensor.matmul, nc.tensor.transpose
            ident = F(IDENT, P)
            waited = set()

            def once(s, n):
                if (s.name, n) not in waited:
                    waited.add((s.name, n))
                    pe.wait_ge(s, n)

            def once_copied(s):
                bank, n = use[s]
                once(free[bank], n + 1)

            def do(s):
                kind = s[0]
                if kind == "ao":
                    h, i = s[1:]
                    bank = use[s][0]
                    if i == 0 and h:
                        pe.wait_ge(free[7], h)
                else:
                    bank = take_bank(pe, s)
                last = None
                if kind == "xT":
                    t, q = s[1:]
                    once(consts_in, 32)
                    once(x_scaled, t + 1)
                    for c in range(4):
                        last = tr(B(bank, [(1, P)], off=c * P), V(H0 + t * D + 4 * q + c, [(KD, P)]), ident)
                elif kind == "ab":
                    once(disc_done, 1)
                    for i, r in enumerate((10, 11, 14, 15)):
                        last = tr(B(bank, [(1, NQ)], off=i * NQ), F(DS + r * P, P, 0, NQ), F(IDENT, NQ, 0, NQ))
                elif kind == "cT":
                    once(cnat_in, 64)
                    tiles = [(s[1], t) for t in range(4)] if s[1] < 2 else [(0, 4), (1, 4)]
                    for i, (ri, t) in enumerate(tiles):
                        last = tr(B(bank, [(1, P)], off=i * P), F(CNAT + ri * 640 + t * P, P), ident)
                elif kind == "rb":
                    once(params_in, 16 * 12)
                    last = mm(B(bank, [(1, 320)], 0, AH), F(RELB, AH, 0, 32), F(OH + s[1] * 320, 320, 0, 32),
                              start=True, stop=True)
                elif kind == "pj":
                    i = chunk_no[s[1:]]
                    slot = RING[i % NW]
                    pe.wait_ge(chunk_in[i % NW], 16 * (i // NW + 1))
                    if s[1] == "glu":
                        once(z_ready, NB5)
                        for k in range(5):
                            last = mm(B(bank, [(1, S)]), F(slot + k * P, P), F(ZT + k * S, S),
                                      start=(k == 0), stop=(k == 4))
                    elif s[1] in ("ih", "gh", "va", "wo"):
                        lhs = X0
                        if s[1] == "wo":
                            lhs = M0
                            once_copied(("az", AH - 1))
                            once_copied(("hz", HH - 1))
                            once(s5_mixed, NB5)
                        for t in range(TB):
                            for k in range(KD):
                                last = mm(B(bank, [(1, P)], off=t * P), F(lhs + k * S + t * P, P), F(slot + k * P, P),
                                          start=(k == 0), stop=(k == KD - 1))
                    else:
                        for q in range(16):
                            once_copied(("xT", q // 4, q % 4))
                        for k in range(KD):
                            last = mm(B(bank, [(1, S)]), F(slot + k * P, P), F(X0 + k * S, S),
                                      start=(k == 0), stop=(k == KD - 1))
                elif kind == "w1T":
                    b, ri = s[1:]
                    once(w1_ready, 2 * b + 2)
                    for q in range(QB):
                        last = tr(B(bank, [(1, P)], off=q * P), F(W1 + ri * 512 + q * P, P), ident)
                elif kind == "kk":
                    b, half = s[1:]
                    once(ca_ready, 2 * b + 2)
                    for i in range(4):
                        q, p0 = i, SN * half
                        for ri in range(2):
                            last = mm(B(bank, [(1, P)], 0, SC, off=i * P),
                                      F(BB + ri * 320 + (QB * b + q) * SC, SC, p0, SN),
                                      F(CA + ri * 576 + q * 144, P, p0, SN), start=(ri == 0), stop=(ri == 1))
                elif kind == "st":
                    b = s[1]
                    for ri in range(2):
                        once_copied(("w1T", b, ri))
                    once(up_in, 16 * LC * (b + 1))
                    for gq in range(8):
                        q, p0 = gq // 2, SN * (gq % 2)
                        for ri in range(2):
                            last = mm(B(bank, [(1, NC5)], p0, SN, off=ri * 256 + q * NC5),
                                      F(W1T + ri * 512 + q * P + p0, SN), F(UP + gq * NC5, NC5),
                                      start=True, stop=True)
                elif kind == "y5":
                    b, par = s[1:]
                    once(t_ready, 16 * LC * (b + 1))
                    once(scanned, b + 1)
                    for q in range(4):
                        gq = 2 * q + par
                        mm(B(bank, [(1, NC5)], off=q * NC5), F(S5T + gq * P, P), F(UP + gq * NC5, NC5),
                           start=True, stop=False)
                        for ri in range(2):
                            last = mm(B(bank, [(1, NC5 - 1)], off=q * NC5 + 1),
                                      F(CA + ri * 576 + q * 144 + SC, P, par * SN, SN),
                                      F(SX + ri * 256 + q * NC5, NC5 - 1, par * SN, SN), start=False, stop=(ri == 1))
                elif kind == "hs":
                    l, h = s[1:]
                    once(level_ready, l + 1)
                    for t in range(TB):
                        last = mm(B(bank, [(1, P)], off=t * P), F(KT + h * S + t * P, P), F(QT + h * S + t * P, P),
                                  start=True, stop=True)
                elif kind == "hk":
                    once(level_ready, 9)
                    for t in range(3):
                        last = tr(B(bank, [(1, P)], off=t * P), F(KT + s[1] * S + t * P, P), ident)
                elif kind == "hu":
                    h = s[1]
                    once_copied(("hk", h))
                    for t in range(3):
                        last = mm(B(bank, [(1, P)], off=t * P), F(HKN + (h % 2) * 384 + t * P, P),
                                  F(VH + t * 640 + h * P, P), start=True, stop=True)
                elif kind == "ho":
                    h = s[1]
                    once_copied(("hu", h))
                    for t in range(TB):
                        last = mm(B(bank, [(1, P)], off=t * P), F(HAT + h * S + t * P, P), F(VH + t * 640 + h * P, P),
                                  start=True, stop=(t == 0))
                        if t:
                            last = mm(B(bank, [(1, P)], off=t * P), F(QT + h * S + t * P, P),
                                      F(HS + (h * 3 + t - 1) * P, P), start=False, stop=True)
                elif kind == "hz":
                    h = s[1]
                    once(ho_ready, h + 1)
                    for t in range(TB):
                        last = tr(B(bank, [(1, P)], off=t * P), F(GH + t * 640 + h * P, P), ident)
                elif kind == "al":
                    h, i, m = s[1:]
                    for j in range(AH):
                        for k in ("qa", "ka", "va"):
                            once_copied(("pj", k, j))
                    n = (i + 1) * P
                    last = mm(B(bank, [(1, n)]), F(AQ + h * S + i * P, P, m * QK, QK), F(AK + h * S, n, m * QK, QK),
                              start=True, stop=True)
                elif kind == "aw":
                    h, i = s[1:]
                    u = h * TB + i
                    pe.wait_ge(w_ready, u + 1)
                    for t in range(i + 1):
                        last = tr(B(bank, [(1, P)], off=t * P), F(AW[u % 2] + t * P, P), ident)
                elif kind == "ao":
                    u = h * TB + i
                    once_copied(("aw", h, i))
                    for t in range(i + 1):
                        last = mm(B(bank, [(1, P)], off=i * P), F(AWT[u % 2] + t * P, P), F(AVV + t * 768 + h * P, P),
                                  start=(t == 0), stop=(t == i))
                elif kind == "az":
                    once(ao_ready, s[1] + 1)
                    for t in range(TB):
                        last = tr(B(bank, [(1, P)], off=t * P), F(AO + t * P, P), ident)
                elif kind == "hT":
                    t, q = s[1:]
                    once(hs_ready, t + 1)
                    for c in range(4):
                        last = tr(B(bank, [(1, P)], off=c * P), V(HSB + (t % 2) * D + 4 * q + c, [(KD, P)]), ident)
                elif kind == "rt":
                    for q in range(16):
                        once_copied(("hT", q // 4, q % 4))
                    for t in range(TB):
                        for k in range(KD):
                            last = mm(B(bank, [(1, 36)], off=t * 36), F(M0 + k * S + t * P, P), F(WR + k * 36, 36),
                                      start=(k == 0), stop=(k == KD - 1))
                elif kind == "rk":
                    once(onehots_ready, 1)
                    for t in range(TB + 1):
                        for u in range(min(t + 1, TB)):
                            last = mm(B(bank, [(1, NE)], off=t * NE), F(C["tri"] if u == t else C["ones"], P),
                                      F(AS + u * NE, NE), start=(u == 0), stop=(u == min(t, TB - 1)))
                elif kind == "id":
                    once(list_in, 16)
                    last = tr(B(bank, [(1, NT)], 0, CAP), F(LSI, CAP, 0, NT), F(IDENT, NT, 0, NT))
                if kind != "ao" or s[2] == TB - 1:
                    last.then_inc(full[bank], 1)

            for s in steps:
                do(s)

            for bank in range(8):
                pe.wait_ge(free[bank], uses[bank])

            def turn(n, par, first):
                pe.wait_ge(rows_in, 16 * (n + 1))
                for f in range(4):
                    if not (first and f < 2):
                        pe.wait_ge(xT_free, 4 * n + f - 1)
                    for c in range(4):
                        last = tr(B(f % 2, [(1, CAP)], off=c * CAP), V(XG + 4 * f + c, [(KD, P)], 0, CAP),
                                  F(IDENT, CAP, 0, CAP))
                    last.then_inc(xT_full, 1)

            def tile(n, par, parts):
                pe.wait_ge(xT_free, 4 * n + 4)
                for which, bank in ((0, 2), (2, 3)):
                    pe.wait_ge(silu_done if which == 0 else h_done, n + 1)
                    for m in range(FT2):
                        for c in range(KD):
                            slot, before = parts[which + c // 8]
                            if m == 0 and c % 8 == 0:
                                pe.wait_ge(slot_in[slot], 16 * (before + 1))
                            last = mm(B(bank, [(1, CAP)], off=m * CAP), F(SLOT[slot] + (c % 8) * FE + m * P, P),
                                      F(XT[par] + c * CAP, CAP), start=(c == 0), stop=(c == KD - 1))
                            if m == FT2 - 1 and c % 8 == 7:
                                last.then_inc(slot_used[slot], 1)
                turn(n + 1, 1 - par, False)
                pe.wait_ge(h_done, n + 2)
                for q in range(4):
                    pe.wait_ge(y_act if q % 2 == 0 else y_dve, 2 * n + 1)
                    for m in range(FT2):
                        slot, before = parts[4 + m // 2]
                        if q == 0 and m % 2 == 0:
                            pe.wait_ge(slot_in[slot], 16 * (before + 1))
                        last = mm(B(4 + q, [(1, 512)], 0, CAP), F(HTE + m * CAP, CAP),
                                  F(SLOT[slot] + (m % 2) * D + q * 512, 512), start=(m == 0), stop=(m == FT2 - 1))
                        if q == 3 and m % 2 == 1:
                            last.then_inc(slot_used[slot], 1)
                    if q < 3:
                        last.then_inc(y_full, 1)

            turn(0, 0, True)
            with pe.Fori(0, NE // 4) as it:
                for k in range(4):
                    tile(it * 4 + k, k % 2, [main_part(it, k, j) for j in range(6)])
            flag = pe.value_load(F(EID + NOV, 1, 0, 1).bitcast(I32), min_val=0, max_val=NOV)
            with pe.If(flag > 0):
                with pe.Fori(0, NOV // 2) as it:
                    for k in range(2):
                        tile(it * 2 + k + NE, k % 2, [over_part(it, k, j) for j in range(6)])

        @block.scalar
        def _(act):
            A = nc.scalar.activation

            def evac(s, dst, dims, func=ACT.Copy, **kw):
                bank = see_bank(act, s)
                A(dst, B(bank, dims[0], *dims[1:]), func, **kw).then_inc(free[bank], 1)

            n_step = [0]

            def deviation(srcs, junk, ss, sd, width, scales=None):
                for i, x in enumerate(srcs):
                    kw = {} if scales is None else {"scale": F(scales + i, 1)}
                    A(junk, x, ACT.Square, accum_out=F(ss + i, 1), **kw).then_inc(act_step, 1)
                    n_step[0] += 1
                    act.wait_ge(act_step, n_step[0])
                return A(F(sd, len(srcs)), F(ss, len(srcs)), ACT.Sqrt, scale=1.0 / width, bias=F(EPSC, 1))

            act.wait_ge(eps_set, 1)
            for t in range(TB):
                act.wait_ge(x_in[t], 16)
                deviation([F(H0 + t * D, D)], F(X0 + t * D, D), SSQ + t, STD + t, D).then_inc(x_std, 1)
            act.wait_ge(disc_in, 48)
            A(V(DS + 2 * P, [(SN, 2), (1, SN)], 0, NQ), V(LDT, [(1, 2), (0, SN)], 0, NQ), ACT.Exp).then_inc(disc_act, 1)
            act.wait_ge(disc_dve, 1)
            A(F(DS + 3 * P, P, 0, NQ), F(DS + 3 * P, P, 0, NQ), ACT.Exp).then_inc(disc_act, 1)
            act.wait_ge(lb_dve, 1)
            A(F(LBE, HH), F(LB, HH), ACT.Exp).then_inc(lb_act, 1)
            act.wait_ge(lam_dve, 1)
            A(F(LAME, 2), F(LAMD, 2), ACT.Exp).then_inc(lam_act, 1)
            act.wait_ge(disc_dve, 2)
            A(F(DS + 7 * P, P, 0, NQ), F(DS + 6 * P, P, 0, NQ), ACT.Sin)
            A(F(DS + 8 * P, P, 0, NQ), F(DS + 6 * P, P, 0, NQ), ACT.Sin, scale=0.5).then_inc(disc_act, 1)

            def do(s):
                kind = s[0]
                if kind == "pj":
                    k, j = s[1:]
                    if k == "u":
                        evac(s, V(UT + j * S, [(NC5, LC), (1, NC5)]), ([(1, LC), (LC, NC5)],))
                    elif k == "fh":
                        bank = see_bank(act, s)
                        A(F(FT + j * S, S), B(bank, [(1, S)]), ACT.Sigmoid)
                        A(F(KT + j * S, S), B(bank, [(1, S)]), ACT.Sigmoid, scale=-1.0).then_inc(free[bank], 1)
                    elif k == "qh":
                        evac(s, F(QT + j * S, S), ([(1, S)],), ACT.Silu)
                    elif k == "ih":
                        if j == 0:
                            see_copy(act, ("cT", 2))
                            act.wait_ge(bias_out, 16)
                            act.wait_ge(lam_dve, 2)
                        evac(s, V(VH + j * P, [(640, TB), (1, P)]), ([(P, TB), (1, P)],))
                    elif k == "gh":
                        if j == 0:
                            act.wait_ge(ca_ready, 2 * NB5)
                        evac(s, V(GH + j * P, [(640, TB), (1, P)]), ([(P, TB), (1, P)],), ACT.Sigmoid)
                    elif k in ("qa", "ka"):
                        if k == "qa" and j == 0:
                            act.wait_ge(s5_mixed, NB5)
                        evac(s, F((AQ if k == "qa" else AK) + j * S, S), ([(1, S)],))
                    elif k == "va":
                        evac(s, V(AVV + j * P, [(768, TB), (1, P)]), ([(P, TB), (1, P)],))
                    elif k == "glu":
                        if j >= 2:
                            act.wait_ge(s5_mixed, j - 1)
                        evac(s, F(ST + (j % 2) * S, S), ([(1, S)],), ACT.Sigmoid)
                elif kind == "w1T":
                    b, ri = s[1:]
                    evac(s, F(W1T + ri * 512, 512), ([(1, 512)],))
                elif kind == "kk":
                    b, half = s[1:]
                    if b:
                        act.wait_ge(t_ready, 16 * LC * b)
                    evac(s, V(KBUF + half * P, [(2 * P, 4), (1, P)], 0, SC), ([(P, 4), (1, P)], 0, SC))
                elif kind == "y5":
                    b, par = s[1:]
                    if b:
                        act.wait_ge(y_out, 16 * LC * b)
                    evac(s, V(YP + par * NC5, [(2 * NC5, 4), (1, NC5)]), ([(NC5, 4), (1, NC5)],))
                elif kind == "hk":
                    h = s[1]
                    if h >= 2:
                        see_bank(act, ("hu", h - 2))
                    evac(s, F(HKN + (h % 2) * 384, 384), ([(1, 384)],))
                elif kind == "ho":
                    h = s[1]
                    bank = see_bank(act, s)
                    if h:
                        act.wait_ge(ho_ready, h)
                    deviation([B(bank, [(1, P)], off=t * P) for t in range(TB)], F(HSQ, P), SM + 16, HST,
                              HD).then_inc(ho_std, 1)
                elif kind == "ao" and s[2] == TB - 1:
                    h = s[1]
                    act.wait_ge(full[7], h + 1)
                    act.wait_ge(w_ready, TB * (h + 1))
                    if h:
                        act.wait_ge(ao_ready, h)
                    deviation([B(7, [(1, P)], off=t * P) for t in range(TB)], F(ASQ, P), SM + 20, HST + TB, AV,
                              R0 + (h % 2) * TB).then_inc(ao_std, 1)
                elif kind == "hz":
                    evac(s, F(M0 + (11 + s[1]) * S, S), ([(1, S)],), scale=F(HNG, 1))
                elif kind == "al" and s[3] == 1:
                    u = s[1] * TB + s[2]
                    n = (s[2] + 1) * P
                    act.wait_ge(l_ready, u + 1)
                    for m in range(2):
                        x = F(AL[u % 2] + m * 512, n)
                        last = A(x, x, ACT.Exp, bias=F(SM + (u % 2) * 8 + m, 1), accum_out=F(SM + (u % 2) * 8 + 2 + m, 1))
                    last.then_inc(e_ready, 1)
                elif kind == "aw":
                    u = s[1] * TB + s[2]
                    n = (s[2] + 1) * P
                    evac(s, F(AWT[u % 2], n), ([(1, n)],))
                elif kind == "az":
                    if s[1] == 0:
                        act.wait_ge(s5_mixed, NB5)
                    evac(s, F(M0 + s[1] * S, S), ([(1, S)],), scale=F(SUBG, 1))
                elif kind == "hT":
                    t, q = s[1:]
                    evac(s, V(M0 + 4 * q * S + t * P, [(S, 4), (1, P)]), ([(P, 4), (1, P)],))

            def gelu(b):
                act.wait_ge(yT_sum, b + 1)
                A(F(ZT + b * S, S), F(YT, S), ACT.Gelu_apprx_tanh).then_inc(z_ready, 1)

            for s in steps:
                if s == ("hT", 0, 0):
                    for j in range(16):
                        see_copy(act, ("pj", "wo", j))
                    for t in range(TB):
                        deviation([F(H0 + t * D, D)], F(JUNK, D), SSQ + t, STD + t, D).then_inc(h_std, 1)
                do(s)
                if s[0] == "pj" and s[1:] in GELU_AFTER:
                    gelu(GELU_AFTER[s[1:]])
            act.wait_ge(groups_diff, 1)
            A(F(RGE, 16), F(RGD, 16), ACT.Exp).then_inc(groups_exp, 1)
            act.wait_ge(gates_diff, 1)
            A(F(RE2, TB), F(RDF, TB), ACT.Exp).then_inc(gates_exp, 1)

            def tile(n, parts):
                slot, before = parts[1]
                act.wait_ge(slot_used[slot], before + 2)
                act.wait_ge(h_done, n + 1)
                A(F(SIL, 4 * CAP), B(2, [(1, 4 * CAP)]), ACT.Silu).then_inc(silu_done, 1)
                for q in (0, 2):
                    act.wait_ge(y_full, 3 * n + q + 1)
                    act.wait_ge(ysb_free, n + 1)
                    A(F(YSB + q * 512, 512, 0, CAP), B(4 + q, [(1, 512)], 0, CAP), ACT.Copy).then_inc(y_act, 1)

            with act.Fori(0, NE // 4) as it:
                for k in range(4):
                    tile(it * 4 + k, [main_part(it, k, j) for j in range(6)])
            act.wait_ge(slots_ready, 1)
            flag = act.value_load(F(EID + NOV, 1, 0, 1).bitcast(I32), min_val=0, max_val=NOV)
            with act.If(flag > 0):
                with act.Fori(0, NOV // 2) as it:
                    for k in range(2):
                        tile(it * 2 + k + NE, [over_part(it, k, j) for j in range(6)])
            for t in range(TB):
                act.wait_ge(sum_ready, t + 1)
                deviation([F(H0 + t * D, D)], F(A0 + D * (2 + 2 * t), D), SSQ + t, STD + t, D).then_inc(sum_std, 1)

        @block.vector
        def _(dve):
            v = nc.vector
            n_step = [0]

            def put(ins):
                n_step[0] += 1
                ins.then_inc(dve_step, 1)

            def settle(ins=None):
                if ins is not None:
                    put(ins)
                dve.wait_ge(dve_step, n_step[0])

            def tt(o, a, b, op):
                return v.tensor_tensor(o, a, b, op)

            def ts(o, a, s1, s2, op0, op1=None):
                return v.tensor_scalar(o, a, s1, s2, op0, op1) if op1 is not None else v.tensor_scalar(o, a, s1, None, op0)

            M, AD, SU = ALU.mult, ALU.add, ALU.subtract
            v.memset(F(EPSC, 1), EPS).then_inc(eps_set, 1)
            for t in range(TB):
                dve.wait_ge(x_std, t + 1)
                settle(v.reciprocal(F(RST + t, 1), F(STD + t, 1)))
                ts(F(H0 + t * D, D), F(H0 + t * D, D), F(RST + t, 1), None, M).then_inc(x_scaled, 1)

            def R(i):
                return F(DS + i * P, P, 0, NQ)

            def disc_a():
                dve.wait_ge(disc_in, 48)
                settle(ts(R(0), R(0), -1e-4, None, ALU.min))
                dve.wait_ge(disc_act, 1)
                put(tt(R(4), R(1), R(2), M))
                tt(R(3), R(0), R(2), M).then_inc(disc_dve, 1)
                settle()
                settle(ts(R(5), R(4), 1.0 / (2 * math.pi), 12582912.0, M, AD))
                settle(ts(R(5), R(5), 12582912.0, None, SU))
                settle(v.scalar_tensor_tensor(R(6), R(5), -6.28125, R(4), M, AD))
                settle(v.scalar_tensor_tensor(R(6), R(5), -(2 * math.pi - 6.28125), R(6), M, AD))
                ts(R(6), R(6), 3.1415925, -3.1415925, ALU.min, ALU.max).then_inc(disc_dve, 1)
                dve.wait_ge(params_in, 16 * 12)
                tt(F(LB, HH), F(LBL, HH), F(LBL, HH), SU).then_inc(lb_dve, 1)
                tt(V(LAMP, [(SN, 2), (1, SN)]), V(LAML, [(128, 2), (1, SN)]), V(LAML + SN, [(128, 2), (1, SN)]),
                   M).then_inc(dve_step, 1)
                n_step[0] += 1
                settle()
                v.tensor_reduce(F(LAMD, 2), V(LAMP, [(SN, 2), (1, SN)]), AX.X, AD).then_inc(lam_dve, 1)
                settle(ts(F(SUBG, 1), F(SUB, 1), 1.0 - LAM_INIT, None, M))

            def disc_b():
                dve.wait_ge(disc_act, 3)
                settle(tt(R(9), R(8), R(8), M))
                settle(ts(R(9), R(9), -2.0, 1.0, M, AD))
                put(tt(R(10), R(3), R(9), M))
                settle(tt(R(11), R(3), R(7), M))
                put(ts(R(12), R(10), 1.0, None, SU))
                put(tt(R(5), R(0), R(0), M))
                settle(tt(R(6), R(1), R(1), M))
                settle(tt(R(13), R(5), R(6), AD))
                put(v.reciprocal(R(13), R(13)))
                put(tt(R(5), R(12), R(0), M))
                put(tt(R(6), R(11), R(1), M))
                put(tt(R(7), R(11), R(0), M))
                settle(tt(R(8), R(12), R(1), M))
                put(tt(R(5), R(5), R(6), AD))
                settle(tt(R(7), R(7), R(8), SU))
                put(tt(R(14), R(5), R(13), M))
                tt(R(15), R(7), R(13), M).then_inc(disc_done, 1)
                settle()
                dve.wait_ge(lb_act, 1)
                settle(v.reciprocal(F(LBR, HH), F(LBE, HH)))
                settle(tt(F(LBE, HH), F(LBE, HH), F(LBR, HH), M))
                settle(tt(F(LB, HH), F(LBE, HH), F(LBE, HH), SU))
                settle(ts(F(LB1, HH), F(LB, HH), -1.0, 1.0, M, AD))
                dve.wait_ge(lam_act, 1)
                settle(ts(F(NLAM, 1), F(LAME + 1, 1), -LAM_INIT, None, AD))
                settle(tt(F(NLAM, 1), F(NLAM, 1), F(LAME, 1), SU))
                v.nop().then_inc(lam_dve, 1)

            def cmul(o, a, b, dims_o, dims_a, dims_b, n):
                t = [F(ST + 256 * i, n) for i in range(4)]

                def shaped(x, dims):
                    st = 1
                    out_ = []
                    for _, c in reversed(dims):
                        out_.append((st, c))
                        st *= c
                    return V(x, list(reversed(out_)))

                for i, (x, y) in enumerate(((0, 0), (1, 1), (0, 1), (1, 0))):
                    put(tt(shaped(ST + 256 * i, dims_a), V(a[x], dims_a), V(b[y], dims_b), M))
                settle()
                put(tt(V(o[0], dims_o), shaped(ST, dims_a), shaped(ST + 256, dims_a), SU))
                settle(tt(V(o[1], dims_o), shaped(ST + 512, dims_a), shaped(ST + 768, dims_a), AD))

            def tables():
                bank = see_bank(dve, ("ab",))
                put(v.tensor_copy(F(PW + NQ, NQ), B(bank, [(1, NQ)])))
                put(v.tensor_copy(F(PW + 180 + NQ, NQ), B(bank, [(1, NQ)], off=NQ)))
                v.tensor_copy(F(FRI, 2 * NQ), B(bank, [(1, 2 * NQ)], off=2 * NQ)).then_inc(free[bank], 1)
                dve.wait_ge(free[bank], use[("ab",)][1] + 1)
                put(v.memset(F(PW, NQ), 1.0))
                put(v.memset(F(PW + 180, NQ), 0.0))
                settle()
                p = (PW, PW + 180)
                for n in (1, 2, 4):
                    cmul([x + (n + 1) * NQ for x in p], [x + NQ for x in p], [x + n * NQ for x in p],
                         [(NQ, n), (1, NQ)], [(NQ, n), (1, NQ)], [(0, n), (1, NQ)], n * NQ)
                settle(ts(F(PW + 360, 180), F(PW + 180, 180), -1.0, None, M))
                for x in range(2):
                    for j in range(LC):
                        put(v.tensor_copy(F(PR + x * 160 + j * NQ, NQ), F(PW + x * 180 + (7 - j) * NQ, NQ)))
                    put(v.tensor_copy(F(SP + x * 120, NQ), F(PW + x * 180 + 8 * NQ, NQ)))
                settle()
                for l in range(1, 6):
                    a = [SP + x * 120 + (l - 1) * NQ for x in range(2)]
                    cmul([x + NQ for x in a], a, a, [(1, NQ)], [(1, NQ)], [(1, NQ)], NQ)
                for q0 in (0, 10):
                    cmul([BB + x * 320 + q0 * SC for x in range(2)], [BRAW + x * 320 + q0 * SC for x in range(2)],
                         [FRI + x * NQ + q0 for x in range(2)],
                         [(SC, 10), (1, SC)], [(SC, 10), (1, SC)], [(1, 10), (0, SC)], 160)
                for i in range(3):
                    s = ("cT", i)
                    bank = see_bank(dve, s)
                    tiles = [(i, 0, 4, 0)] if i < 2 else [(0, 4, 1, 0), (1, 4, 1, P)]
                    for ri, t0, nt, off in tiles:
                        for par in range(2):
                            for t in range(nt):
                                last = v.tensor_copy(
                                    V(CRI + ri * 320 + (t0 + t) * 4 * SC, [(SC, 4), (1, SC)], par * SN, SN),
                                    B(bank, [(2 * SC, 4), (1, SC)], par * SN, SN, off=off + t * P + par * SC))
                                if not (ri == tiles[-1][0] and par == 1 and t == nt - 1):
                                    put(last)
                    last.then_inc(free[bank], 1)
                    dve.wait_ge(free[bank], use[s][1] + 1)
                settle()
                v.nop().then_inc(tables_ready, 1)
                for i in range(2):
                    s = ("rb", i)
                    bank = see_bank(dve, s)
                    tt(F(RR + i * 320, 320, 0, AH), B(bank, [(1, 320)], 0, AH), F(RM + i * 320, 320, 0, AH),
                       AD).then_inc(free[bank], 1)
                    dve.wait_ge(free[bank], use[s][1] + 1)
                v.nop().then_inc(bias_row, 1)

            def scan(b):
                s = ("st", b)
                bank = see_bank(dve, s)
                if b:
                    see_bank(dve, ("y5", b - 1, 1))
                v.tensor_copy(F(SX, 512), B(bank, [(1, 512)])).then_inc(free[bank], 1)
                dve.wait_ge(free[bank], use[s][1] + 1)
                for l in range(6):
                    sh = 1 << l
                    n = NC5 - sh
                    x = [V(SX + r * 256, [(NC5, QB), (1, n)]) for r in range(2)]
                    a = [V(SP + r * 120 + l * NQ + QB * b, [(1, QB), (0, n)]) for r in range(2)]
                    t = [V(ST + 256 * i, [(NC5, QB), (1, n)]) for i in range(4)]
                    for i, (p, q) in enumerate(((0, 0), (1, 1), (0, 1), (1, 0))):
                        put(tt(t[i], a[p], x[q], M))
                    settle()
                    put(tt(t[0], t[0], t[1], SU))
                    settle(tt(t[2], t[2], t[3], AD))
                    y = [V(SX + r * 256 + sh, [(NC5, QB), (1, n)]) for r in range(2)]
                    put(tt(y[0], y[0], t[0], AD))
                    settle(tt(y[1], y[1], t[2], AD))
                v.nop().then_inc(scanned, 1)

            def skip(b):
                dve.wait_ge(yT_in, 16 * (b + 1))
                v.scalar_tensor_tensor(F(YT, S), F(UT + b * S, S), F(D5 + b, 1), F(YT, S), M, AD).then_inc(yT_sum, 1)

            def hgrn_prepare():
                for k in ("fh", "qh", "gh"):
                    for j in range(HH):
                        see_copy(dve, ("pj", k, j))
                for h in range(HH):
                    put(ts(F(FT + h * S, S), F(FT + h * S, S), F(LB1 + h, 1), F(LB + h, 1), M, AD))
                    put(ts(F(KT + h * S, S), F(KT + h * S, S), F(LB1 + h, 1), None, M))
                settle(ts(F(QT, HH * S), F(QT, HH * S), HD ** -0.5, None, M))
                v.nop().then_inc(level_ready, 1)

            def level(l):
                if l == 0:
                    dve.wait_ge(s5_mixed, NB5)
                for h in range(HH):
                    s = ("hs", l, h)
                    bank = see_bank(dve, s)
                    o = V(HAT + h * S, [(P, TB), (1, P)])
                    x = B(bank, [(P, TB), (1, P)])
                    if l == 0:
                        tt(o, x, V(IDENT, [(0, TB), (1, P)]), M).then_inc(free[bank], 1)
                    else:
                        v.copy_predicated(o, V(C[f"mask{LEVELS[l - 1]}"], [(0, TB), (1, P)]).bitcast(U32),
                                          x).then_inc(free[bank], 1)
                dve.wait_ge(free[bank], use[s][1] + 1)
                if l == 0:
                    settle(tt(F(QT, HH * S), F(QT, HH * S), F(FT, HH * S), M))
                else:
                    L = LEVELS[l - 1]
                    n2 = HH * S // (2 * L)
                    src = FT if l % 2 == 1 else HT2
                    dst = TOT if l == 7 else (HT2 if l % 2 == 1 else FT)
                    put(tt(V(QT + L, [(2 * L, n2), (1, L)]), V(QT + L, [(2 * L, n2), (1, L)]),
                           V(src, [(2, n2), (0, L)]), M))
                    put(tt(V(KT, [(2 * L, n2), (1, L)]), V(KT, [(2 * L, n2), (1, L)]),
                           V(src + 1, [(2, n2), (0, L)]), M))
                    settle(tt(F(dst, n2), V(src, [(2, n2)]), V(src + 1, [(2, n2)]), M))
                v.nop().then_inc(level_ready, 1)

            def hgrn_states(h):
                s = ("hu", h)
                bank = see_bank(dve, s)
                x = [F(HS + (h * 3 + t) * P, P) for t in range(3)]
                settle(v.tensor_copy(x[0], B(bank, [(1, P)])))
                settle(v.scalar_tensor_tensor(x[1], x[0], F(TOT + h * TB + 1, 1), B(bank, [(1, P)], off=P), M, AD))
                v.scalar_tensor_tensor(x[2], x[1], F(TOT + h * TB + 2, 1), B(bank, [(1, P)], off=2 * P), M,
                                       AD).then_inc(free[bank], 1)

            def hgrn_out(h):
                s = ("ho", h)
                bank = see_bank(dve, s)
                dve.wait_ge(ho_std, h + 1)
                settle(v.reciprocal(F(HST, TB), F(HST, TB)))
                tt(V(HO, [(P, TB), (1, P)]), B(bank, [(P, TB), (1, P)]), V(HST, [(1, TB), (0, P)]),
                   M).then_inc(free[bank], 1)
                dve.wait_ge(free[bank], use[s][1] + 1)
                gate = V(GH + h * P, [(640, TB), (1, P)])
                tt(gate, gate, V(HO, [(P, TB), (1, P)]), M).then_inc(ho_ready, 1)
                dve.wait_ge(ho_ready, h + 1)

            def logits(u):
                h, i = units[u]
                n = (i + 1) * P
                if i == 0:
                    dve.wait_ge(strip_in[h % 2], 16 * (h // 2 + 1))
                for m in range(2):
                    s = ("al", h, i, m)
                    bank = see_bank(dve, s)
                    v.scalar_tensor_tensor(F(AL[u % 2] + m * 512, n), B(bank, [(1, n)]), QK ** -0.5,
                                           F(STRIP + (h % 2) * 512 + 512 - n, n), M, AD).then_inc(free[bank], 1)
                for m in range(2):
                    bank, c = use[("al", h, i, m)]
                    dve.wait_ge(free[bank], c + 1)
                if i == TB - 1:
                    v.nop().then_inc(strip_used, 1)
                sm = SM + (u % 2) * 8
                settle(v.tensor_reduce(F(sm, 2), V(AL[u % 2], [(512, 2), (1, n)]), AX.X, ALU.max))
                ts(F(sm, 2), F(sm, 2), -1.0, None, M).then_inc(l_ready, 1)

            def weights(u):
                h, i = units[u]
                n = (i + 1) * P
                sm = SM + (u % 2) * 8
                dve.wait_ge(e_ready, u + 1)
                put(v.reciprocal(F(R0 + (h % 2) * TB + i, 1), F(sm + 2, 1)))
                settle(v.reciprocal(F(sm + 4, 1), F(sm + 3, 1)))
                settle(ts(F(sm + 4, 1), F(sm + 4, 1), F(sm + 2, 1), F(NLAM, 1), M, M))
                if u >= 2:
                    see_bank(dve, ("aw",) + units[u - 2])
                v.scalar_tensor_tensor(F(AW[u % 2], n), F(AL[u % 2] + 512, n), F(sm + 4, 1), F(AL[u % 2], n), M,
                                       AD).then_inc(w_ready, 1)
                dve.wait_ge(w_ready, u + 1)

            def attn_out(h):
                s = ("ao", h, TB - 1)
                bank = 7
                dve.wait_ge(full[7], h + 1)
                if h:
                    see_bank(dve, ("az", h - 1))
                dve.wait_ge(ao_std, h + 1)
                settle(v.reciprocal(F(HST + TB, TB), F(HST + TB, TB)))
                settle(tt(F(HST + TB, TB), F(HST + TB, TB), F(R0 + (h % 2) * TB, TB), M))
                tt(V(AO, [(P, TB), (1, P)]), B(bank, [(P, TB), (1, P)]), V(HST + TB, [(1, TB), (0, P)]),
                   M).then_inc(free[7], 1)
                dve.wait_ge(free[7], h + 1)
                v.nop().then_inc(ao_ready, 1)

            def do(s):
                kind = s[0]
                if kind == "xT":
                    t, q = s[1:]
                    if (t, q) == (0, 0):
                        dve.wait_ge(consts_in, 32)
                        dve.wait_ge(x_scaled, TB)
                    bank = see_bank(dve, s)
                    tt(V(X0 + 4 * q * S + t * P, [(S, 4), (1, P)]), B(bank, [(P, 4), (1, P)]),
                       V(GMIX + 4 * q, [(1, 4), (0, P)]), M).then_inc(free[bank], 1)
                    if (t, q) == (1, 3):
                        disc_a()
                    if (t, q) == (3, 3):
                        disc_b()
                elif kind == "rb" and s[1] == 1:
                    tables()
                elif kind == "st":
                    scan(s[1])
                elif kind == "pj" and s[1:] in GELU_AFTER:
                    skip(GELU_AFTER[s[1:]])
                elif s == ("pj", "gh", HH - 1):
                    hgrn_prepare()
                elif kind == "pj" and s[1] == "glu":
                    j = s[2]
                    see_copy(dve, s)
                    tt(V(MS5 + j * S, [(1, LC), (LC, NC5)]), V(ST + (j % 2) * S, [(NC5, LC), (1, NC5)]),
                       V(ZT + j * S, [(NC5, LC), (1, NC5)]), M).then_inc(s5_mixed, 1)
                elif kind == "hs" and s[2] == HH - 1:
                    level(s[1])
                elif kind == "hu":
                    hgrn_states(s[1])
                elif kind == "ho":
                    hgrn_out(s[1])
                elif kind == "al" and s[3] == 1:
                    u = s[1] * TB + s[2]
                    if u == 0:
                        see_bank(dve, ("hz", HH - 1))
                    logits(u)
                    if u >= 1:
                        weights(u - 1)
                    if u >= 5 and u % TB == 1:
                        attn_out(u // TB - 1)
                elif s == ("az", AH - 1):
                    weights(len(units) - 1)
                    attn_out(AH - 1)
                elif kind == "pj" and s[1] == "wo":
                    j = s[2]
                    if j == 0:
                        dve.wait_ge(x_again, 16 * TB)
                    bank = see_bank(dve, s)
                    o = V(H0 + j * P, [(D, TB), (1, P)])
                    tt(o, B(bank, [(P, TB), (1, P)]), o, AD).then_inc(free[bank], 1)
                elif kind == "hT" and s[2] == 0:
                    t = s[1]
                    if t == 0:
                        dve.wait_ge(gf_in, 16)
                    dve.wait_ge(h_std, t + 1)
                    settle(v.reciprocal(F(RST + t, 1), F(STD + t, 1)))
                    if t >= 2:
                        dve.wait_ge(hs_out[t % 2], 16)
                        for q in range(4):
                            see_bank(dve, ("hT", t - 2, q))
                    v.scalar_tensor_tensor(F(HSB + (t % 2) * D, D), F(H0 + t * D, D), F(RST + t, 1), F(GF, D), M,
                                           M).then_inc(hs_ready, 1)

            for s in steps:
                do(s)

            s = ("rt",)
            bank = see_bank(dve, s)
            dve.wait_ge(h_std, TB)
            v.tensor_copy(F(RLG, 144), B(bank, [(1, 144)])).then_inc(free[bank], 1)
            dve.wait_ge(free[bank], use[s][1] + 1)
            v.memset(F(LSI, CAP, 0, NT), SENT).then_inc(list_clear, 1)
            gl, el = V(RLG, [(36, TB), (1, NGRP)]), V(RLG + 4, [(36, TB), (1, NE)])

            def first_max(x, n, mx, oh, tmp, cm):
                settle(v.tensor_reduce(F(mx, TB), x, AX.X, ALU.max))
                settle(tt(V(tmp, [(n, TB), (1, n)]), x, V(mx, [(1, TB), (0, n)]), ALU.is_equal))
                settle(tt(V(tmp, [(n, TB), (1, n)]), V(tmp, [(n, TB), (1, n)]), V(C["rev"], [(0, TB), (1, n)]), M))
                settle(v.tensor_reduce(F(cm, TB), V(tmp, [(n, TB), (1, n)]), AX.X, ALU.max))
                settle(tt(V(oh, [(n, TB), (1, n)]), V(tmp, [(n, TB), (1, n)]), V(cm, [(1, TB), (0, n)]), ALU.is_equal))

            first_max(gl, NGRP, RGM, ROG, RTMP, RCM)
            tt(V(RGD, [(4, TB), (1, 4)]), gl, V(RGM, [(1, TB), (0, 4)]), SU).then_inc(groups_diff, 1)
            settle(ts(F(ROG, 16), F(ROG, 16), 1.0, BIG, SU, M))
            settle(tt(V(REL, [(NE, TB), (EPG, NGRP), (1, EPG)]), V(RLG + 4, [(36, TB), (EPG, NGRP), (1, EPG)]),
                      V(ROG, [(4, TB), (1, NGRP), (0, EPG)]), AD))
            ex = V(REL, [(NE, TB), (1, NE)])
            first_max(ex, NE, RV1, RO1, RTMP, RCM)
            settle(v.scalar_tensor_tensor(F(REL, 128), F(RO1, 128), -BIG, F(REL, 128), M, AD))
            first_max(ex, NE, RV2, RO2, RTMP, RCM)
            tt(F(RDF, TB), F(RV2, TB), F(RV1, TB), SU).then_inc(gates_diff, 1)
            settle(tt(F(AS, 128), F(RO1, 128), F(RO2, 128), AD))
            v.nop().then_inc(onehots_ready, 1)
            dve.wait_ge(groups_exp, 1)
            settle(v.tensor_reduce(F(RGS, TB), V(RGE, [(4, TB), (1, 4)]), AX.X, AD))
            put(v.reciprocal(F(RGS, TB), F(RGS, TB)))
            dve.wait_ge(gates_exp, 1)
            settle(ts(F(RDF, TB), F(RE2, TB), 1.0, None, AD))
            settle(v.reciprocal(F(RDF, TB), F(RDF, TB)))
            settle(tt(F(GATE, TB), F(RGS, TB), F(RDF, TB), M))
            settle(tt(F(GATE + TB, TB), F(GATE, TB), F(RE2, TB), M))
            s = ("rk",)
            bank = see_bank(dve, s)
            settle(v.tensor_copy(F(RCN, NE), B(bank, [(1, NE)], off=TB * NE)))
            settle(ts(F(RNV, NE), F(RCN, NE), float(CAP), None, ALU.is_gt))
            for j in range(2, (S - 1) // CAP + 1):
                settle(v.scalar_tensor_tensor(F(RNV, NE), F(RCN, NE), float(CAP * j), F(RNV, NE), ALU.is_gt, AD))
            settle(v.tensor_tensor_scan(F(RCU, NE), F(C["ones"], NE), F(RNV, NE), 0.0, M, AD))
            settle(tt(F(ROB, NE), F(RCU, NE), F(RNV, NE), SU))
            settle(v.scalar_tensor_tensor(F(ROB, NE), F(ROB, NE), float(CAP), F(C["over"], NE), M, AD))
            rk = B(bank, [(NE, TB), (1, NE)])
            all3 = [(NE, TB), (1, NE)]
            settle(ts(V(RTMP, all3), rk, float(CAP), None, ALU.is_ge))
            settle(tt(V(RTMP, all3), V(RTMP, all3), V(ROB, [(0, TB), (1, NE)]), M))
            tt(V(REL, all3), rk, V(C["base"], [(0, TB), (1, NE)]), AD).then_inc(free[bank], 1)
            dve.wait_ge(free[bank], use[s][1] + 1)
            settle(tt(F(REL, 128), F(REL, 128), F(RTMP, 128), AD))
            for k, oh in enumerate((RO1, RO2)):
                settle(tt(F(RTMP, 128), F(oh, 128), F(REL, 128), M))
                settle(v.tensor_reduce(F(RPF + k * TB, TB), V(RTMP, all3), AX.X, AD))
                put(ts(F(IDS + k * TB, TB), F(C["tok"], TB), float(k * S), None, AD))
            v.tensor_copy(F(POSU, 2 * TB).bitcast(U32), F(RPF, 2 * TB)).then_inc(dve_step, 1)
            n_step[0] += 1
            settle()
            v.nop().then_inc(pos_ready, 1)
            settle(tt(V(RBG, [(NE, NOV), (1, NE)]), V(RCU, [(0, NOV), (1, NE)]), V(C["ovi"], [(1, NOV), (0, NE)]),
                      ALU.is_le))
            settle(v.tensor_reduce(F(REI, NOV), V(RBG, [(NE, NOV), (1, NE)]), AX.X, AD))
            settle(ts(F(REI, NOV), F(REI, NOV), float(NE - 1), None, ALU.min))
            settle(v.tensor_copy(F(REI + NOV, 1), F(RCU + NE - 1, 1)))
            settle(v.tensor_copy(F(EID, NOV + 1).bitcast(I32), F(REI, NOV + 1)))
            settle(v.memset(F(SLOTF, NT + 1), SENT))
            s = ("id",)
            bank = see_bank(dve, s)
            v.tensor_copy(F(SLOTF, NT, 0, CAP), B(bank, [(1, NT)], 0, CAP)).then_inc(free[bank], 1)
            dve.wait_ge(free[bank], use[s][1] + 1)
            settle(v.tensor_copy(F(DSTU, NT + 1).bitcast(U32), F(SLOTF, NT + 1)))
            settle(ts(F(TOKU, NT + 1), F(SLOTF, NT + 1), float(S), -float(S), ALU.is_ge, M))
            settle(tt(F(SLOTF, NT + 1), F(SLOTF, NT + 1), F(TOKU, NT + 1), AD))
            settle(v.tensor_copy(F(TOKU, NT + 1).bitcast(U32), F(SLOTF, NT + 1)))
            v.nop().then_inc(slots_ready, 1)

            def turned(n, par):
                for f in range(4):
                    dve.wait_ge(xT_full, 4 * n + f + 1)
                    v.tensor_copy(F(XT[par] + 4 * f * CAP, 4 * CAP), B(f % 2, [(1, 4 * CAP)])).then_inc(xT_free, 1)

            def tile(n, par, parts):
                slot, before = parts[3]
                dve.wait_ge(slot_used[slot], before + 2)
                dve.wait_ge(silu_done, n + 2)
                tt(F(HTE, 4 * CAP), F(SIL, 4 * CAP), B(3, [(1, 4 * CAP)]), M).then_inc(h_done, 1)
                turned(n + 1, 1 - par)
                dve.wait_ge(y_full, 3 * n + 2)
                dve.wait_ge(ysb_free, n + 1)
                v.tensor_copy(F(YSB + 512, 512, 0, CAP), B(5, [(1, 512)], 0, CAP)).then_inc(y_dve, 1)
                slot, before = parts[5]
                dve.wait_ge(slot_used[slot], before + 2)
                v.tensor_copy(F(YSB + 3 * 512, 512, 0, CAP), B(7, [(1, 512)], 0, CAP)).then_inc(y_dve, 1)

            turned(0, 0)
            with dve.Fori(0, NE // 4) as it:
                for k in range(4):
                    tile(it * 4 + k, k % 2, [main_part(it, k, j) for j in range(6)])
            flag = dve.value_load(F(EID + NOV, 1, 0, 1).bitcast(I32), min_val=0, max_val=NOV)
            with dve.If(flag > 0):
                with dve.Fori(0, NOV // 2) as it:
                    for k in range(2):
                        tile(it * 2 + k + NE, k, [over_part(it, k, j) for j in range(6)])

            for t in range(TB):
                dve.wait_ge(fin_in[t], 32)
                x = F(H0 + t * D, D)
                settle(v.scalar_tensor_tensor(x, F(A0 + D * (1 + 2 * t), D), F(GATE + t, 1), x, M, AD))
                v.scalar_tensor_tensor(x, F(A0 + D * (2 + 2 * t), D), F(GATE + TB + t, 1), x, M, AD).then_inc(sum_ready, 1)
                if t == 0:
                    dve.wait_ge(fg_in, 16)
                dve.wait_ge(sum_std, t + 1)
                settle(v.reciprocal(F(RST + t, 1), F(STD + t, 1)))
                v.scalar_tensor_tensor(F(A0 + D * (1 + 2 * t), D), x, F(RST + t, 1), F(A0, D), M, M).then_inc(out_ready, 1)


_IN = ["x", "w_in", "w_out", "mix_norm_g", "ffn_norm_g", "rel_bias", "diff_lambda", "attn_subln_g", "s5_a_re",
       "s5_a_im", "s5_log_dt", "s5_b_re", "s5_b_im", "s5_c_re", "s5_c_im", "s5_d", "s5_w_glu", "hgrn_lb_logits",
       "hgrn_norm_g", "moe_w_group", "moe_w_router", "moe_w_gate", "moe_w_up", "moe_w_down", "final_norm_g"]


def arrays_of(inputs):
    block, cols, onehot, masked = shape_constants()
    arrays = {}
    for name in _IN:
        a = np.ascontiguousarray(inputs[name])
        arrays[name] = a[0] if a.ndim > 1 and a.shape[0] == 1 else a
    arrays.update(consts=block, onehot=onehot, masked=masked)
    return arrays, cols


def kernel(**inputs):
    import concourse.bacc as _bacc
    from concourse.bass_utils import run_bass_kernel_spmd as _run

    arrays, cols = arrays_of(inputs)
    nc = _bacc.Bacc("TRN2", target_bir_lowering=False, num_devices=1)
    d = {k: nc.dram_tensor(f"in_{k}", a.shape, mybir.dt.from_np(a.dtype), kind="ExternalInput").ap()
         for k, a in arrays.items()}
    out = nc.dram_tensor("out_0", (S, D), F32, kind="ExternalOutput").ap()
    build(nc, d, out, cols)
    r = _run(nc, [{f"in_{k}": a for k, a in arrays.items()}], core_ids=[0])
    return r.results[0]["out_0"].reshape(1, S, D)
```

```python
import math
from contextlib import ExitStack

import numpy as np

import concourse.bass as bass
from concourse import mybir

ALU = mybir.AluOpType
ACT = mybir.ActivationFunctionType
AX = mybir.AxisListType
F32 = mybir.dt.float32
U32 = mybir.dt.uint32
I32 = mybir.dt.int32

P = 128
EPS = 1e-6
D = 2048
S = 512
TB = S // P
KD = D // P
AH, QK, AV = 6, 64, 128
SG, SC, SN = 40, 16, 64
HH, HD = 5, 128
LC = 8
NC5 = S // LC
NB5 = SG // 8
QB = 4
NQ = SG // 2
NE, EPG, NGRP, FE = 32, 8, 4, 512
CAP = 96
NOV = 2 * S // CAP
NT = NE + NOV
SENT = 4096.0
NAS = 2 * TB
BIG = 1.0e30
LAM_INIT = 0.8 - 0.6 * math.exp(-0.3 * 0)
RB = 640
S5_START = 0
LEVELS = [1, 2, 4, 8, 16, 32, 64]
NIN = 5504
COLS = {"qa": 0, "ka": 768, "va": 1536, "u": 2304, "qh": 2944, "fh": 3584, "ih": 4224, "gh": 4864}


def shape_constants():
    i = np.arange(P)
    s, t = i[:, None], i[None, :]
    parts = {
        "ident": (s == t),
        "tri": (s < t),
        "ones": np.ones((P, P)),
    }
    for L in LEVELS:
        parts[f"mask{L}"] = (s // (2 * L) == t // (2 * L)) & (s % (2 * L) < L) & (t % (2 * L) >= L)
    parts["rev"] = np.broadcast_to(NE - np.arange(NE), (P, NE))
    parts["base"] = np.broadcast_to(CAP * np.arange(NT + 1), (P, NT + 1))
    parts["slot"] = np.broadcast_to(np.arange(CAP) - CAP, (P, CAP))
    parts["over"] = np.broadcast_to(CAP * (NE - 1 - np.arange(NE)), (P, NE))
    parts["ovi"] = np.broadcast_to(np.arange(NOV), (P, NOV))
    parts["tok"] = i[:, None] + P * np.arange(TB)[None, :]
    cols, at = {}, 0
    for k, v in parts.items():
        cols[k] = (at, v.shape[1])
        at += v.shape[1]
    block = np.concatenate([np.asarray(v, np.float32) for v in parts.values()], axis=1)
    dist = S - 1 - np.arange(RB)
    n = np.maximum(dist, 0)
    large = 16 + (np.log(np.maximum(n, 1).astype(np.float32) / 16) / math.log(128 / 16) * 16).astype(np.int32)
    bucket = np.where(n < 16, n, np.minimum(large, 31))
    onehot = (bucket[None, :] == np.arange(32)[:, None]).astype(np.float32)
    masked = np.broadcast_to(np.where(dist >= 0, 0.0, -BIG).astype(np.float32), (AH, RB))
    return np.ascontiguousarray(block), cols, np.ascontiguousarray(onehot), np.ascontiguousarray(masked)


def build(nc, d, out, cc):
    ctx = ExitStack()
    with ctx:
        def sem(name):
            return ctx.enter_context(nc.semaphore(name))

        W = 53100
        arena = ctx.enter_context(nc.sbuf_tensor("arena", [P, W], F32))
        abase = arena[:, :]
        psum = ctx.enter_context(nc.psum_tensor("psum", [P, 8 * 512], F32))
        pbase = psum[:, :]

        def V(off, dims, p0=0, n=P):
            return bass.AP(tensor=abase.tensor, offset=p0 * W + off, ap=[[W, n]] + [[s, c] for s, c in dims])

        def F(off, n, p0=0, parts=P):
            return V(off, [(1, n)], p0, parts)

        def B(bank, dims, p0=0, n=P, off=0):
            return bass.AP(tensor=pbase.tensor, offset=p0 * 4096 + bank * 512 + off,
                           ap=[[4096, n]] + [[s, c] for s, c in dims])

        def DV(t, off, dims):
            return bass.AP(tensor=t.tensor, offset=t.offset + off, ap=[[s, c] for s, c in dims])

        at = [0]

        def take(n):
            at[0] += n
            return at[0] - n

        ncon = sum(n for _, n in cc.values())
        CON = take(ncon)
        C = {k: CON + o for k, (o, _) in cc.items()}
        IDENT = C["ident"]
        WR = take(KD * 36)
        GMIX = take(KD)
        LBL, LBE, LBR, LB, LB1, D5 = take(HH), take(HH), take(HH), take(HH), take(HH), take(NB5)
        SUB, SUBG, HNG = take(1), take(1), take(1)
        LAMD, LAME, NLAM = take(2), take(2), take(1)
        FRI = take(2 * NQ)
        SSQ, STD, RST, EPSC = take(TB), take(TB), take(TB), take(1)
        SM = take(24)
        R0 = take(TB * 2)
        HST = take(2 * TB)
        TOT = take(HH * TB)
        GATE = take(2 * TB)
        SLOTF, TOKU, DSTU = take(NT + 2), take(NT + 2), take(NT + 2)
        EID = take(NOV + 1)
        LDT = take(2)
        GIDX, SIDX = [take(1), take(1)], take(1)
        H0 = 2600
        assert at[0] <= H0, at[0]
        A0 = H0 + 8192
        X0 = A0 + 16384
        M0 = X0 + 8192
        E0 = M0 + 8192
        NW, WS = 3, 2048
        RING = [E0 + i * WS for i in range(NW)]
        W1T = E0 + NW * WS
        KBUF = W1T + 1024
        PT = KBUF + 1024
        assert PT + 1152 <= W
        CNAT, OH, RM, RR, LAML, RELB, BRAW, CRI = (A0, A0 + 1280, A0 + 1920, A0 + 2560, A0 + 3200, A0 + 3456,
                                                   A0 + 3600, A0 + 4480)
        DIAG = A0 + 7680
        LAMP = A0 + 4240
        VH, GH = A0, A0 + 2560
        UT, ZT = A0 + 5120, A0 + 7680
        S5T = A0 + 10240
        CA = S5T + 1024
        SX = CA + 1152
        ST = SX + 512
        W1 = ST + 1024
        YP = W1 + 1024
        assert YP + 512 <= X0
        PW = M0
        PR = PW + 540
        SP = PR + 320
        BB = SP + 240
        UP, YT = M0 + 2048, M0 + 2560
        assert BB + 640 <= UP
        DS = M0 + 11 * 512
        MS5 = M0 + 6 * 512
        FT, KT, QT, HO = H0, H0 + 2560, H0 + 5120, H0 + 7680
        AQ, AK = A0 + 5120, A0 + 8192
        HAT = A0 + 11264
        HT2 = HAT + 2560
        STRIP = HT2 + 1280
        assert STRIP + 1024 <= X0
        HS, HKN, HSQ = FT, HT2, HT2 + 768
        AVV = A0
        AL = [HAT, A0 + 3072]
        AW = [HAT + 1024, HAT + 1536]
        AWT = [HAT + 2048, HT2]
        AO, ASQ = A0 + 4096, A0 + 4608
        GF, HSB, JUNK = E0 + 2048, [E0, E0 + 4096], E0 + 6144
        RLT = GF
        RGE_T = E0 + 4096
        ROT = RGE_T + NAS * (NT + 1)
        ROS = ROT + NAS * NT
        assert ROS + NAS * CAP <= E0 + 6144
        at[0] = E0 + 6144
        RLG, RGM, RGD, RGE, ROG, RTMP, RCM, REL = (take(n) for n in (144, 4, 16, 16, 16, 128, 4, 128))
        RV1, RV2, RO1, RO2, RDF, RE2, AS, RGS = (take(n) for n in (4, 4, 128, 128, 4, 4, 128, 4))
        RNV, RCU, ROB, RPF, IDS, RTL, RSL, RBG, REI = (
            take(n) for n in (NE, NE, NE, NAS, NAS, NAS, NAS, NE * NOV, NOV + 1))
        RKS, RPX = take(TB * NE), take((TB + 1) * NE)
        SSP = take(TB * 16)
        assert at[0] <= W
        EIDV = F(EID, NOV + 1, 0, 1).bitcast(I32)
        TOKV, DSTV = F(TOKU, NT + 2).bitcast(U32), F(DSTU, NT + 2).bitcast(U32)

        def scratch(name, shape):
            return nc.dram_tensor(name, shape, F32, kind="Internal").ap()

        u_d = scratch("u_scratch", [NB5 * P, S])
        y_d = scratch("y_scratch", [NB5 * P, S])
        r_d = scratch("bias_rows", [AH * P, RB])
        hs_d = scratch("hs_rows", [S, D])
        ex_d = scratch("expert_rows", [2 * S, D])

        def quarters(kinds):
            return [[("pq",) + c + (q,)] if q < 3 else [("pj",) + c] for c in kinds for q in range(4)]

        def whole(kind, n):
            return [(kind, j) for j in range(n)]

        gaps = quarters(whole("u", 5))
        gaps[3] += [("ab",), ("cT", 0), ("cT", 1), ("cT", 2), ("rb", 0), ("rb", 1)]
        mid = whole("fh", 5) + whole("qh", 5) + whole("ih", 5) + whole("gh", 5)
        g = quarters(mid)
        for b in range(NB5):
            at_ = 16 * b + S5_START
            for k, s in enumerate(([("w1T", b, 0), ("w1T", b, 1)], [], [("kk", b, 0), ("kk", b, 1)],
                                   [("st", b)], [], [], [], [], [], [("y5", b, 0), ("y5", b, 1)])):
                g[min(at_ + k, len(g) - 1)] += s
        GELU_AFTER = {mid[min(4 * b + 4, len(mid) - 1)]: b for b in range(NB5 - 1)}
        gaps += g
        pre = [(k, j) for j in range(4) for k in ("qa", "ka")]
        g = quarters(pre)
        hg = []
        for l in range(8):
            hg += [[("hs", l, h) for h in range(HH)], []]
        hg += [[("hk", 0), ("hk", 1)], [("hu", 0), ("hk", 2)], [("hu", 1), ("hk", 3)], [("hu", 2), ("hk", 4)],
               [("hu", 3), ("ho", 0)], [("hu", 4), ("ho", 1)], [("ho", 2)], [("ho", 3), ("hz", 0)],
               [("ho", 4), ("hz", 1)], [("hz", 2)], [("hz", 3)], [("hz", 4)]]
        for k, s in enumerate(hg):
            g[k + 2] += s
        gaps += [[s for c in quarters(whole("glu", 5)) for s in c]] + g
        units = [(h, i) for h in range(AH) for i in range(TB)]

        def tick(n):
            out_ = []
            if n < len(units):
                out_ += [("al",) + units[n] + (0,), ("al",) + units[n] + (1,)]
            if 2 <= n < len(units) + 2:
                out_.append(("aw",) + units[n - 2])
            if n >= 3:
                h, i = units[n - 3]
                out_.append(("ao", h, i))
                if i == 1 and h >= 1:
                    out_.append(("az", h - 1))
            return out_

        rest = [("va", 0), ("va", 1), ("va", 2), ("va", 3), ("qa", 4), ("ka", 4), ("va", 4), ("qa", 5), ("ka", 5),
                ("va", 5)]
        done_, n = set(pre), 0
        for gap in quarters(rest):
            if gap[0][0] == "pj":
                done_.add(gap[0][1:])
            ready = n < len(units) + 3 and (n >= len(units) or ("ka", n // TB) in done_) and (
                n < 3 or ("va", (n - 3) // TB) in done_)
            if ready:
                gap += tick(n)
                n += 1
            gaps.append(gap)
        tail = []
        while n < len(units) + 3:
            tail.append(tick(n))
            n += 1
        tail.append([("az", AH - 1)])
        assert len(tail) >= TB
        for q in range(TB):
            tail[len(tail) - TB + q].insert(0, ("pq", "wo", 0, q))
        gaps += tail + [[("pj", "wo", 0)]] + quarters(whole("wo", 16)[1:])
        steps = [("xT", t, q) for t in range(TB) for q in range(4)] + [s for gap in gaps for s in gap]
        steps += [("hT", t, q) for t in range(TB) for q in range(4)]
        steps += [("rt",), ("rT",), ("rk",), ("id",)]
        chunks = [s[1:] for s in steps if s[0] == "pj"]
        chunk_no = {c: i for i, c in enumerate(chunks)}
        use, turns, uses = {}, [0, 0], [0] * 8
        for s in steps:
            if s[0] == "ao":
                use[s] = (7, s[1])
            elif s[0] != "pq":
                big = s[0] == "pj"
                bank = 5 + turns[1] % 2 if big else turns[0] % 5
                turns[big] += 1
                use[s] = (bank, uses[bank])
                uses[bank] += 1
        uses[7] = AH

        full = [sem(f"bank_full{i}") for i in range(8)]
        free = [sem(f"bank_free{i}") for i in range(8)]
        dve_step, pool_step, pool_passed = sem("dve_step"), sem("pool_step"), sem("pool_passed")
        chunk_in = [sem(f"chunk_in{i}") for i in range(NW)]
        consts_in, params_in, disc_in, cnat_in = sem("consts_in"), sem("params_in"), sem("disc_in"), sem("cnat_in")
        strip_in = [sem("strip_in0"), sem("strip_in1")]
        x_in = [sem(f"x_in{i}") for i in range(TB)]
        x_std, x_diag = sem("x_std"), sem("x_diag")
        disc_act, disc_dve, disc_done = sem("disc_act"), sem("disc_dve"), sem("disc_done")
        tables_ready = sem("tables_ready")
        lb_dve, lb_act, lam_dve, lam_act = sem("lb_dve"), sem("lb_act"), sem("lam_dve"), sem("lam_act")
        w1_ready, ca_ready, t_zero, t_ready = sem("w1_ready"), sem("ca_ready"), sem("t_zero"), sem("t_ready")
        up_in, u_out = sem("up_in"), [sem(f"u_out{b}") for b in range(NB5)]
        scanned, y_out, yT_in, yT_sum = sem("scanned"), sem("y_out"), sem("yT_in"), sem("yT_sum")
        z_ready, s5_mixed = sem("z_ready"), sem("s5_mixed")
        level_ready, ho_std, ho_ready = sem("level_ready"), sem("ho_std"), sem("ho_ready")
        bias_row, bias_out, strip_used = sem("bias_row"), sem("bias_out"), sem("strip_used")
        act_step, eps_set, ao_std = sem("act_step"), sem("eps_set"), sem("ao_std")
        l_ready, e_ready, w_ready, ao_ready = sem("l_ready"), sem("e_ready"), sem("w_ready"), sem("ao_ready")
        x_again, h_std, gf_in, hs_ready = sem("x_again"), sem("h_std"), sem("gf_in"), sem("hs_ready")
        hs_out = [sem("hs_out0"), sem("hs_out1")]
        squares_done, squares_sum = sem("squares_done"), sem("squares_sum")
        groups_diff, groups_exp, gates_diff, gates_exp = (
            sem("groups_diff"), sem("groups_exp"), sem("gates_diff"), sem("gates_exp"))
        onehots_ready, places_ready, slots_ready = sem("onehots_ready"), sem("places_ready"), sem("slots_ready")
        slot_in = [sem(f"slot_in{i}") for i in range(8)]
        slot_used = [sem(f"slot_used{i}") for i in range(8)]
        gidx_set, sidx_set, rows_out = sem("gidx_set"), sem("sidx_set"), sem("rows_out")
        rows_in = [sem("rows_in0"), sem("rows_in1")]
        ysb_free = sem("ysb_free")
        xg_clear, xT_full, xT_free = sem("xg_clear"), sem("xT_full"), sem("xT_free")
        silu_done, h_done, y_full, y_act, y_dve = (
            sem("silu_done"), sem("h_done"), sem("y_full"), sem("y_act"), sem("y_dve"))
        moe_done, fin_in, fg_in = sem("moe_done"), [sem(f"fin_in{i}") for i in range(TB)], sem("fg_in")
        sum_ready, sum_std, out_ready, out_done = (
            sem("sum_ready"), sem("sum_std"), sem("out_ready"), sem("out_done"))

        def take_bank(pe, s):
            bank, n = use[s]
            if n:
                pe.wait_ge(free[bank], n)
            return bank

        def see_bank(eng, s):
            bank, n = use[s]
            eng.wait_ge(full[bank], n + 1)
            return bank

        def see_copy(eng, s):
            bank, n = use[s]
            eng.wait_ge(free[bank], n + 1)

        SLOT = [A0 + i * 4096 for i in range(8)]
        XG, YSB, XT = [E0, E0 + 2048], E0 + 4096, E0 + 6144
        HTE = XT + KD * CAP
        SIL = HTE + 4 * CAP
        assert SIL + 4 * CAP <= W
        FT2 = FE // P
        TURN_BANK = (0, 1, 6, 7)

        def main_part(it, k, j):
            L = 6 * k + j
            return L % 8, it * 3 + L // 8

        def over_part(it, k, j):
            return j, 24 + it * 2 + k

        wg_d, wu_d, wd_d = d["moe_w_gate"], d["moe_w_up"], d["moe_w_down"]

        block = ctx.enter_context(nc.Block())

        @block.sync
        def _(sp):
            for t in range(TB):
                sp.dma_start(F(H0 + t * D, D), DV(d["x"], t * P * D, [(D, P), (1, D)])).then_inc(x_in[t], 16)

            def chunk(i):
                kind, j = chunks[i]
                if i >= NW:
                    see_bank(sp, ("pj",) + chunks[i - NW])
                if kind == "glu":
                    rows, src = 5, DV(d["s5_w_glu"], j * P, [(640, P), (P * 640, 5), (1, P)])
                elif kind == "wo":
                    rows, src = KD, DV(d["w_out"], j * P, [(D, P), (P * D, KD), (1, P)])
                else:
                    rows, src = KD, DV(d["w_in"], COLS[kind] + j * P, [(KD * NIN, P), (NIN, KD), (1, P)])
                sp.dma_start(V(RING[i % NW], [(P, rows), (1, P)]), src).then_inc(chunk_in[i % NW], 16)

            def part(e, place, j):
                slot, n = place
                sp.wait_ge(slot_used[slot], n + 1)
                if j < 4:
                    w = wg_d if j < 2 else wu_d
                    src = w[bass.ds(e, 1), :, :].rearrange("e (p c) n -> p (e c n)", p=P)[:, (j % 2) * 4096:
                                                                                         (j % 2 + 1) * 4096]
                    dst = F(SLOT[slot], 4096)
                else:
                    src = wd_d[bass.ds(e, 1), (j - 4) * 256:(j - 3) * 256, :].rearrange("e (m p) n -> p (e m) n", p=P)
                    dst = V(SLOT[slot], [(D, 2), (1, D)])
                sp.dma_start(dst, src).then_inc(slot_in[slot], 16)

            for i in range(len(chunks)):
                if chunks[i] == ("wo", 0):
                    see_copy(sp, ("hz", HH - 1))
                    for t in range(TB):
                        sp.dma_start(F(H0 + t * D, D),
                                     DV(d["x"], t * P * D, [(D, P), (1, D)])).then_inc(x_again, 16)
                chunk(i)
                if chunks[i][0] == "wo" and NW <= chunks[i][1] < NW + 6:
                    j = chunks[i][1] - NW
                    see_copy(sp, ("az", AH - 1))
                    part(0, main_part(0, 0, j), j)
            assert GF == RING[(len(chunks) - NW) % NW]
            see_bank(sp, ("pj",) + chunks[-NW])
            sp.dma_start(F(GF, D), DV(d["ffn_norm_g"], 0, [(0, P), (1, D)])).then_inc(gf_in, 16)
            for t in range(TB):
                sp.wait_ge(hs_ready, t + 1)
                sp.dma_start(DV(hs_d, t * P * D, [(D, P), (1, D)]), F(HSB[t % 2], D)).then_inc(hs_out[t % 2], 16)

            see_bank(sp, ("rt",))
            def later(it, k, j):
                slot, n = main_part(it, k + 1, j)
                return slot, n

            with sp.Fori(0, (NE - 4) // 4) as it:
                for k in range(4):
                    for j in range(6):
                        part(it * 4 + (k + 1), later(it, k, j), j)
            for k in range(3):
                for j in range(6):
                    part(NE - 3 + k, later((NE - 4) // 4, k, j), j)
            sp.wait_ge(slots_ready, 1)
            flag = sp.value_load(F(EID + NOV, 1, 0, 1).bitcast(I32), min_val=0, max_val=NOV)
            with sp.If(flag > 0):
                with sp.Fori(0, NOV // 2) as it:
                    for k in range(2):
                        e = sp.value_load(EIDV[0:1, bass.ds(it * 2 + k, 1)], min_val=0, max_val=NE - 1)
                        for j in range(6):
                            part(e, over_part(it, k, j), j)
            sp.wait_ge(moe_done, 1)
            for t in range(TB):
                if t == 1:
                    sp.dma_start(F(A0, D), DV(d["final_norm_g"], 0, [(0, P), (1, D)])).then_inc(fg_in, 16)
                for k in range(2):
                    sp.dma_start(F(A0 + D * (1 + 2 * t + k), D),
                                 DV(ex_d, (k * S + t * P) * D, [(D, P), (1, D)])).then_inc(fin_in[t], 16)
            for t in range(TB):
                sp.wait_ge(out_ready, t + 1)
                sp.dma_start(DV(out, t * P * D, [(D, P), (1, D)]), F(A0 + D * (1 + 2 * t), D)).then_inc(out_done, 16)
            sp.wait_ge(out_done, 16 * TB)

        @block.gpsimd
        def _(pool):
            g = nc.gpsimd
            for s in slot_used + [silu_done, h_done, y_act, y_dve, ysb_free]:
                pool.sem_inc(s, 1)
            steps_p = [0]

            def settle(ins):
                steps_p[0] += 1
                ins.then_inc(pool_step, 1)
                pool.wait_ge(pool_step, steps_p[0])

            for dst, src in [
                (F(DS, P, 0, NQ), DV(d["s5_a_re"], 0, [(P, NQ), (1, P)])),
                (F(DS + P, P, 0, NQ), DV(d["s5_a_im"], 0, [(P, NQ), (1, P)])),
                (F(LDT, 2, 0, NQ), DV(d["s5_log_dt"], 0, [(2, NQ), (1, 2)])),
            ]:
                pool.dma_start(dst, src, allow_slow_non_contiguous=True).then_inc(disc_in, 16)
            for i, name in enumerate(("s5_c_re", "s5_c_im")):
                for half in range(2):
                    pool.dma_start(V(CNAT + i * 640 + half * SN, [(P, 5), (1, SN)]),
                                   DV(d[name], 0, [(SN, P), (P * SN, 5), (1, SN)])).then_inc(cnat_in, 16)
            for dst, src in [
                (V(BRAW, [(SC, NQ), (1, SC)]), DV(d["s5_b_re"], 0, [(SC, P), (P * SC, NQ), (1, SC)])),
                (V(BRAW + 320, [(SC, NQ), (1, SC)]), DV(d["s5_b_im"], 0, [(SC, P), (P * SC, NQ), (1, SC)])),
                (V(WR, [(36, KD), (1, 4)]), DV(d["moe_w_group"], 0, [(KD * 4, P), (4, KD), (1, 4)])),
                (V(WR + 4, [(36, KD), (1, 32)]), DV(d["moe_w_router"], 0, [(KD * 32, P), (32, KD), (1, 32)])),
                (F(LBL, HH), DV(d["hgrn_lb_logits"], 0, [(1, P), (P, HH)])),
                (F(D5, NB5), DV(d["s5_d"], 0, [(1, P), (P, NB5)])),
                (F(SUB, 1), DV(d["attn_subln_g"], 0, [(1, P), (1, 1)])),
                (F(HNG, 1), DV(d["hgrn_norm_g"], 0, [(1, P), (1, 1)])),
                (F(LAML, 256), DV(d["diff_lambda"], 0, [(0, P), (1, 256)])),
                (F(OH, RB, 0, 32), d["onehot"]),
                (F(RM, RB, 0, AH), d["masked"]),
                (F(RELB, AH, 0, 32), DV(d["rel_bias"], 0, [(AH, 32), (1, AH)])),
            ]:
                pool.dma_start(dst, src, allow_slow_non_contiguous=True).then_inc(params_in, 16)
            g.memset(F(S5T, 1024), 0.0).then_inc(t_zero, 1)
            pool.wait_ge(bias_row, 1)
            pool.dma_start(DV(r_d, 0, [(P * RB, AH), (RB, P), (1, RB)]),
                           V(RR, [(0, P), (1, RB)], 0, AH)).then_inc(bias_out, 16)

            def w1(b):
                for ri in range(2):
                    br, bi = (0, 1) if ri == 0 else (1, 0)
                    pw = [V(PR + x * 160 + QB * b, [(1, QB), (NQ, LC), (0, SC)]) for x in range(2)]
                    bb = [V(BB + x * 320 + QB * b * SC, [(SC, QB), (0, LC), (1, SC)]) for x in (br, bi)]
                    prod = [V(PT + x * 576, [(P, QB), (SC, LC), (1, SC)]) for x in range(2)]
                    g.tensor_tensor(prod[0], pw[0], bb[0], ALU.mult)
                    settle(g.tensor_tensor(prod[1], pw[1], bb[1], ALU.mult))
                    g.tensor_tensor(F(W1 + ri * 512, 512), F(PT, 512), F(PT + 576, 512),
                                    ALU.subtract if ri == 0 else ALU.add).then_inc(w1_ready, 1)
                    pool.wait_ge(w1_ready, 2 * b + ri + 1)

            def ca(b):
                for ri in range(2):
                    pw = [V(PW + x * 180 + QB * b, [(1, QB), (NQ, 9), (0, SC)]) for x in ((0, 1) if ri == 0 else (2, 0))]
                    cc_ = [V(CRI + x * 320 + QB * b * SC, [(SC, QB), (0, 9), (1, SC)]) for x in range(2)]
                    prod = [V(PT + x * 576, [(144, QB), (SC, 9), (1, SC)]) for x in range(2)]
                    g.tensor_tensor(prod[0], cc_[0], pw[0], ALU.mult)
                    settle(g.tensor_tensor(prod[1], cc_[1], pw[1], ALU.mult))
                    g.tensor_tensor(F(CA + ri * 576, 576), F(PT, 576), F(PT + 576, 576),
                                    ALU.subtract).then_inc(ca_ready, 1)
                    pool.wait_ge(ca_ready, 2 * b + ri + 1)

            pool.wait_ge(tables_ready, 1)
            w1(0)
            ca(0)
            for b in range(NB5):
                pool.wait_ge(u_out[b], 16)
                if b >= 1:
                    see_bank(pool, ("y5", b - 1, 1))
                for j in range(LC):
                    pool.dma_start(V(UP, [(NC5, 8), (1, NC5)], SC * j, SC),
                                   DV(u_d, b * P * S + j * NC5, [(S, SC), (SC * S, 8), (1, NC5)])).then_inc(up_in, 16)
                if b + 1 < NB5:
                    for ri in range(2):
                        see_bank(pool, ("w1T", b, ri))
                    w1(b + 1)
                for par in range(2):
                    see_copy(pool, ("y5", b, par))
                if b + 1 < NB5:
                    ca(b + 1)
                pool.wait_ge(y_out, 16 * LC * (b + 1))
                if b >= 1:
                    pool.wait_ge(z_ready, b)
                pool.dma_start(F(YT, S), DV(y_d, b * P * S, [(S, P), (1, S)])).then_inc(yT_in, 16)

            pool.wait_ge(bias_out, 16)
            for h in range(AH):
                if h >= 2:
                    pool.wait_ge(strip_used, h - 1)
                pool.dma_start(F(STRIP + (h % 2) * 512, 512),
                               DV(r_d, h * P * RB + P - 1, [(RB - 1, P), (1, 512)])).then_inc(strip_in[h % 2], 16)

            pool.wait_ge(onehots_ready, 1)
            for s in hs_out:
                pool.wait_ge(s, 32)
            for x in XG:
                g.memset(F(x, D, 0, CAP), 0.0).then_inc(xg_clear, 1)
            pool.wait_ge(xg_clear, 2)
            pool.wait_ge(slots_ready, 1)
            sent = [0]

            def gather(n, par):
                idx = F(GIDX[par], 1, 0, CAP).bitcast(U32)
                g.tensor_copy(idx, TOKV[0:CAP, bass.ds(n, 1)]).then_inc(gidx_set, 1)
                pool.wait_ge(gidx_set, n + 1)
                pool.sem_inc(pool_passed, 1)
                g.indirect_dma_start(out=F(XG[par], D, 0, CAP), out_offset=None, in_=hs_d[:, :],
                                     in_offset=bass.IndirectOffsetOnAxis(ap=idx, axis=0),
                                     bounds_check=S - 1, oob_is_err=False).then_inc(rows_in[par], 16)

            def tile(n, par):
                pool.wait_ge(xT_full, 4 * n + 4)
                gather(n + 2, par)
                g.tensor_copy(F(SIDX, 1, 0, CAP).bitcast(U32), DSTV[0:CAP, bass.ds(n, 1)]).then_inc(sidx_set, 1)
                pool.wait_ge(sidx_set, n + 1)
                pool.wait_ge(y_act, 2 * n + 3)
                pool.wait_ge(y_dve, 2 * n + 3)
                pool.sem_inc(pool_passed, 1)
                g.indirect_dma_start(out=ex_d[:, :], out_offset=bass.IndirectOffsetOnAxis(
                    ap=F(SIDX, 1, 0, CAP).bitcast(U32), axis=0), in_=F(YSB, D, 0, CAP), in_offset=None,
                    bounds_check=2 * S - 1, oob_is_err=False).then_inc(rows_out, 16)
                pool.wait_ge(rows_out, 16 * n + 16)
                pool.sem_inc(ysb_free, 1)

            gather(0, 0)
            gather(1, 1)
            with pool.Fori(0, NE // 2) as it:
                for k in range(2):
                    tile(it * 2 + k, k)
            flag = pool.value_load(F(EID + NOV, 1, 0, 1).bitcast(I32), min_val=0, max_val=NOV)
            with pool.If(flag > 0):
                with pool.Fori(0, NOV // 2) as it:
                    for k in range(2):
                        tile(it * 2 + k + NE, k)
            pool.sem_inc(moe_done, 1)

        @block.tensor
        def _(pe):
            mm, tr = nc.tensor.matmul, nc.tensor.transpose
            ident = F(IDENT, P)
            waited = set()

            def once(s, n):
                if (s.name, n) not in waited:
                    waited.add((s.name, n))
                    pe.wait_ge(s, n)

            def once_copied(s):
                bank, n = use[s]
                once(free[bank], n + 1)

            EARLY = [k for k in range(KD) if k not in (AH - 2, AH - 1)]

            def chunk_quarter(kind, j, quarter):
                s = ("pj", kind, j)
                i = chunk_no[s[1:]]
                slot = RING[i % NW]
                bank = use[s][0]
                if quarter == 0:
                    take_bank(pe, s)
                    pe.wait_ge(chunk_in[i % NW], 16 * (i // NW + 1))
                if kind in ("ih", "gh", "va", "wo"):
                    lhs = X0
                    if kind == "wo":
                        lhs = M0
                        once_copied(("hz", HH - 1))
                        once(s5_mixed, NB5)
                        if j == 0 and quarter < TB:
                            for h in range(AH - 2):
                                once_copied(("az", h))
                            for k in EARLY:
                                mm(B(bank, [(1, P)], off=quarter * P), F(lhs + k * S + quarter * P, P),
                                   F(slot + k * P, P), start=(quarter == 0 and k == EARLY[0]), stop=False,
                                   skip_group_check=True)
                            return
                        for h in (AH - 2, AH - 1):
                            once_copied(("az", h))
                        if j == 0:
                            for k in (AH - 2, AH - 1):
                                for t in range(TB):
                                    last = mm(B(bank, [(1, P)], off=t * P), F(lhs + k * S + t * P, P),
                                              F(slot + k * P, P), start=False, stop=(k == AH - 1),
                                              skip_group_check=True)
                            last.then_inc(full[bank], 1)
                            return
                    for k in range(KD):
                        last = mm(B(bank, [(1, P)], off=quarter * P), F(lhs + k * S + quarter * P, P),
                                  F(slot + k * P, P), start=(k == 0), stop=(k == KD - 1))
                else:
                    n, rhs = (5, ZT) if kind == "glu" else (KD, X0)
                    if kind == "glu":
                        once(z_ready, NB5)
                    else:
                        for q in range(16):
                            once_copied(("xT", q // 4, q % 4))
                    lo, hi = (0, n) if kind == "glu" and quarter == 3 else (quarter * 4, quarter * 4 + 4)
                    if kind == "glu" and quarter < 3:
                        return
                    for k in range(lo, hi):
                        last = mm(B(bank, [(1, S)]), F(slot + k * P, P), F(rhs + k * S, S),
                                  start=(k == 0), stop=(k == n - 1))
                if quarter == 3:
                    last.then_inc(full[bank], 1)

            def do(s):
                kind = s[0]
                if kind == "ao":
                    h, i = s[1:]
                    bank = use[s][0]
                    if i == 0 and h:
                        pe.wait_ge(free[7], h)
                elif kind in ("pq", "pj"):
                    chunk_quarter(s[1], s[2], s[3] if kind == "pq" else 4 if s[1:] == ("wo", 0) else 3)
                    return
                else:
                    bank = take_bank(pe, s)
                last = None
                if kind == "xT":
                    t, q = s[1:]
                    once(x_diag, t + 1)
                    for c in range(4):
                        last = mm(B(bank, [(1, P)], off=c * P), V(H0 + t * D + 4 * q + c, [(KD, P)]),
                                  F(DIAG + t * P, P), start=True, stop=True)
                elif kind == "ab":
                    once(disc_done, 1)
                    for i, r in enumerate((10, 11, 14, 15)):
                        last = tr(B(bank, [(1, NQ)], off=i * NQ), F(DS + r * P, P, 0, NQ), F(IDENT, NQ, 0, NQ))
                elif kind == "cT":
                    once(cnat_in, 64)
                    tiles = [(s[1], t) for t in range(4)] if s[1] < 2 else [(0, 4), (1, 4)]
                    for i, (ri, t) in enumerate(tiles):
                        last = tr(B(bank, [(1, P)], off=i * P), F(CNAT + ri * 640 + t * P, P), ident)
                elif kind == "rb":
                    once(params_in, 16 * 12)
                    last = mm(B(bank, [(1, 320)], 0, AH), F(RELB, AH, 0, 32), F(OH + s[1] * 320, 320, 0, 32),
                              start=True, stop=True)
                elif kind == "w1T":
                    b, ri = s[1:]
                    once(w1_ready, 2 * b + 2)
                    for q in range(QB):
                        last = tr(B(bank, [(1, P)], off=q * P), F(W1 + ri * 512 + q * P, P), ident)
                elif kind == "kk":
                    b, half = s[1:]
                    once(ca_ready, 2 * b + 2)
                    for i in range(4):
                        q, p0 = i, SN * half
                        for ri in range(2):
                            last = mm(B(bank, [(1, P)], 0, SC, off=i * P),
                                      F(BB + ri * 320 + (QB * b + q) * SC, SC, p0, SN),
                                      F(CA + ri * 576 + q * 144, P, p0, SN), start=(ri == 0), stop=(ri == 1))
                elif kind == "st":
                    b = s[1]
                    for ri in range(2):
                        once_copied(("w1T", b, ri))
                    once(up_in, 16 * LC * (b + 1))
                    for gq in range(8):
                        q, p0 = gq // 2, SN * (gq % 2)
                        for ri in range(2):
                            last = mm(B(bank, [(1, NC5)], p0, SN, off=ri * 256 + q * NC5),
                                      F(W1T + ri * 512 + q * P + p0, SN), F(UP + gq * NC5, NC5),
                                      start=True, stop=True)
                elif kind == "y5":
                    b, par = s[1:]
                    once(t_ready, 16 * LC * (b + 1))
                    once(scanned, b + 1)
                    for q in range(4):
                        gq = 2 * q + par
                        mm(B(bank, [(1, NC5)], off=q * NC5), F(S5T + gq * P, P), F(UP + gq * NC5, NC5),
                           start=True, stop=False)
                        for ri in range(2):
                            last = mm(B(bank, [(1, NC5 - 1)], off=q * NC5 + 1),
                                      F(CA + ri * 576 + q * 144 + SC, P, par * SN, SN),
                                      F(SX + ri * 256 + q * NC5, NC5 - 1, par * SN, SN), start=False, stop=(ri == 1))
                elif kind == "hs":
                    l, h = s[1:]
                    once(level_ready, l + 1)
                    for t in range(TB):
                        last = mm(B(bank, [(1, P)], off=t * P), F(KT + h * S + t * P, P), F(QT + h * S + t * P, P),
                                  start=True, stop=True)
                elif kind == "hk":
                    once(level_ready, 9)
                    for t in range(3):
                        last = tr(B(bank, [(1, P)], off=t * P), F(KT + s[1] * S + t * P, P), ident)
                elif kind == "hu":
                    h = s[1]
                    once_copied(("hk", h))
                    for t in range(3):
                        last = mm(B(bank, [(1, P)], off=t * P), F(HKN + (h % 2) * 384 + t * P, P),
                                  F(VH + t * 640 + h * P, P), start=True, stop=True)
                elif kind == "ho":
                    h = s[1]
                    once_copied(("hu", h))
                    for t in range(TB):
                        last = mm(B(bank, [(1, P)], off=t * P), F(HAT + h * S + t * P, P), F(VH + t * 640 + h * P, P),
                                  start=True, stop=(t == 0))
                        if t:
                            last = mm(B(bank, [(1, P)], off=t * P), F(QT + h * S + t * P, P),
                                      F(HS + (h * 3 + t - 1) * P, P), start=False, stop=True)
                elif kind == "hz":
                    h = s[1]
                    once(ho_ready, h + 1)
                    for t in range(TB):
                        last = tr(B(bank, [(1, P)], off=t * P), F(GH + t * 640 + h * P, P), ident)
                elif kind == "al":
                    h, i, m = s[1:]
                    once_copied(("pj", "qa", h))
                    once_copied(("pj", "ka", h))
                    n = (i + 1) * P
                    last = mm(B(bank, [(1, n)]), F(AQ + h * S + i * P, P, m * QK, QK), F(AK + h * S, n, m * QK, QK),
                              start=True, stop=True)
                elif kind == "aw":
                    h, i = s[1:]
                    u = h * TB + i
                    pe.wait_ge(w_ready, u + 1)
                    for t in range(i + 1):
                        last = tr(B(bank, [(1, P)], off=t * P), F(AW[u % 2] + t * P, P), ident)
                elif kind == "ao":
                    u = h * TB + i
                    once_copied(("pj", "va", h))
                    once_copied(("aw", h, i))
                    for t in range(i + 1):
                        last = mm(B(bank, [(1, P)], off=i * P), F(AWT[u % 2] + t * P, P), F(AVV + t * 768 + h * P, P),
                                  start=(t == 0), stop=(t == i))
                elif kind == "az":
                    once(ao_ready, s[1] + 1)
                    for t in range(TB):
                        last = tr(B(bank, [(1, P)], off=t * P), F(AO + t * P, P), ident)
                elif kind == "hT":
                    t, q = s[1:]
                    once(hs_ready, t + 1)
                    for c in range(4):
                        last = tr(B(bank, [(1, P)], off=c * P), V(HSB[t % 2] + 4 * q + c, [(KD, P)]), ident)
                elif kind == "rt":
                    for q in range(16):
                        once_copied(("hT", q // 4, q % 4))
                    for k in range(KD):
                        last = mm(B(bank, [(1, S)], 0, 36), F(WR + k * 36, 36), F(M0 + k * S, S),
                                  start=(k == 0), stop=(k == KD - 1))
                elif kind == "rT":
                    once_copied(("rt",))
                    for t in range(TB):
                        last = tr(B(bank, [(1, 36)], off=t * 36), F(RLT + t * P, P, 0, 36), F(IDENT, 36, 0, 36))
                elif kind == "rk":
                    once(onehots_ready, 1)
                    for i, w in enumerate(("tri", "ones")):
                        last = mm(B(bank, [(1, TB * NE)], off=i * TB * NE), F(C[w], P), F(AS, TB * NE),
                                  start=True, stop=True)
                elif kind == "id":
                    once(places_ready, 1)
                    for c in range(NAS):
                        last = mm(B(bank, [(1, NT)], 0, CAP), F(ROS + c * CAP, CAP), F(ROT + c * NT, NT),
                                  start=(c == 0), stop=(c == NAS - 1))
                if kind != "ao" or s[2] == TB - 1:
                    last.then_inc(full[bank], 1)

            for s in steps:
                do(s)

            for bank in range(8):
                pe.wait_ge(free[bank], uses[bank])

            def turn(n, par, pair, first):
                pe.wait_ge(rows_in[par], 16 * (pair + 1))
                for f in range(4):
                    if f == 2 and not first:
                        pe.wait_ge(y_act, 2 * n - 1)
                        pe.wait_ge(y_dve, 2 * n - 1)
                    for c in range(4):
                        last = tr(B(TURN_BANK[f], [(1, CAP)], off=c * CAP), V(XG[par] + 4 * f + c, [(KD, P)], 0, CAP),
                                  F(IDENT, CAP, 0, CAP))
                    last.then_inc(xT_full, 1)

            def tile(n, par, pair, parts):
                pe.wait_ge(xT_free, 4 * n + 4)
                for which, bank in ((0, 2), (2, 3)):
                    pe.wait_ge(silu_done if which == 0 else h_done, n + 1)
                    for c in range(KD):
                        slot, before = parts[which + c // 8]
                        if c % 8 == 0:
                            pe.wait_ge(slot_in[slot], 16 * (before + 1))
                        for m in range(FT2):
                            last = mm(B(bank, [(1, CAP)], off=m * CAP), F(SLOT[slot] + (c % 8) * FE + m * P, P),
                                      F(XT + c * CAP, CAP), start=(c == 0 and m == 0), stop=(c == KD - 1),
                                      skip_group_check=True)
                        if c % 8 == 7:
                            last.then_inc(slot_used[slot], 1)
                turn(n + 1, 1 - par, pair + par, False)
                pe.wait_ge(h_done, n + 2)
                for m in range(FT2):
                    slot, before = parts[4 + m // 2]
                    if m % 2 == 0:
                        pe.wait_ge(slot_in[slot], 16 * (before + 1))
                    for q in range(4):
                        if m == 0:
                            pe.wait_ge(y_act if q % 2 == 0 else y_dve, 2 * n + 1)
                            if q >= 2:
                                pe.wait_ge(xT_free, 4 * n + q + 5)
                        last = mm(B(4 + q, [(1, 512)], 0, CAP), F(HTE + m * CAP, CAP),
                                  F(SLOT[slot] + (m % 2) * D + q * 512, 512), start=(m == 0), stop=(m == FT2 - 1))
                        if q == 3 and m % 2 == 1:
                            last.then_inc(slot_used[slot], 1)
                        elif m == FT2 - 1:
                            last.then_inc(y_full, 1)

            turn(0, 0, 0, True)
            with pe.Fori(0, NE // 4) as it:
                for k in range(4):
                    tile(it * 4 + k, k % 2, it * 2 + k // 2, [main_part(it, k, j) for j in range(6)])
            flag = pe.value_load(F(EID + NOV, 1, 0, 1).bitcast(I32), min_val=0, max_val=NOV)
            with pe.If(flag > 0):
                with pe.Fori(0, NOV // 2) as it:
                    for k in range(2):
                        tile(it * 2 + k + NE, k, it + NE // 2, [over_part(it, k, j) for j in range(6)])

        @block.scalar
        def _(act):
            A = nc.scalar.activation

            def evac(s, dst, dims, func=ACT.Copy, **kw):
                bank = see_bank(act, s)
                A(dst, B(bank, dims[0], *dims[1:]), func, **kw).then_inc(free[bank], 1)

            n_step = [0]

            def deviation(srcs, junk, ss, sd, width, scales=None):
                for i, x in enumerate(srcs):
                    kw = {} if scales is None else {"scale": F(scales + i, 1)}
                    A(junk, x, ACT.Square, accum_out=F(ss + i, 1), **kw).then_inc(act_step, 1)
                    n_step[0] += 1
                    act.wait_ge(act_step, n_step[0])
                return A(F(sd, len(srcs)), F(ss, len(srcs)), ACT.Sqrt, scale=1.0 / width, bias=F(EPSC, 1))

            act.dma_start(F(CON, ncon), d["consts"]).then_inc(consts_in, 16)
            act.dma_start(F(GMIX, KD), DV(d["mix_norm_g"], 0, [(KD, P), (1, KD)])).then_inc(consts_in, 16)
            act.wait_ge(eps_set, 1)
            for t in range(TB):
                act.wait_ge(x_in[t], 16)
                deviation([F(H0 + t * D, D)], F(A0 + 8192, D), SSQ + t, STD + t, D).then_inc(x_std, 1)
            act.wait_ge(disc_in, 48)
            A(V(DS + 2 * P, [(SN, 2), (1, SN)], 0, NQ), V(LDT, [(1, 2), (0, SN)], 0, NQ), ACT.Exp).then_inc(disc_act, 1)
            act.wait_ge(disc_dve, 1)
            A(F(DS + 3 * P, P, 0, NQ), F(DS + 3 * P, P, 0, NQ), ACT.Exp).then_inc(disc_act, 1)
            act.wait_ge(lb_dve, 1)
            A(F(LBE, HH), F(LB, HH), ACT.Exp).then_inc(lb_act, 1)
            act.wait_ge(lam_dve, 1)
            A(F(LAME, 2), F(LAMD, 2), ACT.Exp).then_inc(lam_act, 1)
            act.wait_ge(disc_dve, 2)
            A(F(DS + 7 * P, P, 0, NQ), F(DS + 6 * P, P, 0, NQ), ACT.Sin)
            A(F(DS + 8 * P, P, 0, NQ), F(DS + 6 * P, P, 0, NQ), ACT.Sin, scale=0.5).then_inc(disc_act, 1)

            def do(s):
                kind = s[0]
                if kind == "pj":
                    k, j = s[1:]
                    if k == "u":
                        evac(s, V(UT + j * S, [(NC5, LC), (1, NC5)]), ([(1, LC), (LC, NC5)],))
                        see_copy(act, s)
                        act.dma_start(DV(u_d, j * P * S, [(S, P), (1, S)]), F(UT + j * S, S)).then_inc(u_out[j], 16)
                    elif k == "fh":
                        bank = see_bank(act, s)
                        A(F(FT + j * S, S), B(bank, [(1, S)]), ACT.Sigmoid)
                        A(F(KT + j * S, S), B(bank, [(1, S)]), ACT.Sigmoid, scale=-1.0).then_inc(free[bank], 1)
                    elif k == "qh":
                        evac(s, F(QT + j * S, S), ([(1, S)],), ACT.Silu)
                    elif k == "ih":
                        if j == 0:
                            see_copy(act, ("cT", 2))
                            act.wait_ge(bias_out, 16)
                            act.wait_ge(lam_dve, 2)
                        evac(s, V(VH + j * P, [(640, TB), (1, P)]), ([(P, TB), (1, P)],))
                    elif k == "gh":
                        if j == 0:
                            act.wait_ge(ca_ready, 2 * NB5)
                        evac(s, V(GH + j * P, [(640, TB), (1, P)]), ([(P, TB), (1, P)],), ACT.Sigmoid)
                    elif k in ("qa", "ka"):
                        if k == "qa" and j == 0:
                            act.wait_ge(s5_mixed, NB5)
                        evac(s, F((AQ if k == "qa" else AK) + j * S, S), ([(1, S)],))
                    elif k == "va":
                        evac(s, V(AVV + j * P, [(768, TB), (1, P)]), ([(P, TB), (1, P)],))
                    elif k == "wo":
                        see_copy(act, s)
                        for t in range(TB):
                            if j or t:
                                act.wait_ge(squares_done, j * TB + t)
                            A(F(JUNK, P), F(H0 + t * D + j * P, P), ACT.Square,
                              accum_out=F(SSP + t * 16 + j, 1)).then_inc(squares_done, 1)
                    elif k == "glu":
                        if j >= 2:
                            act.wait_ge(s5_mixed, j - 1)
                        evac(s, F(ST + (j % 2) * S, S), ([(1, S)],), ACT.Sigmoid)
                elif kind == "w1T":
                    b, ri = s[1:]
                    evac(s, F(W1T + ri * 512, 512), ([(1, 512)],))
                elif kind == "kk":
                    b, half = s[1:]
                    if b:
                        act.wait_ge(t_ready, 16 * LC * b)
                    evac(s, V(KBUF + half * P, [(2 * P, 4), (1, P)], 0, SC), ([(P, 4), (1, P)], 0, SC))
                    if half:
                        for x in range(2):
                            see_copy(act, ("kk", b, x))
                        if b == 0:
                            act.wait_ge(t_zero, 1)
                        for j in range(LC):
                            n = P - SC * j
                            act.dma_start(V(S5T + SC * j, [(P, 8), (1, n)], SC * j, SC),
                                          V(KBUF, [(P, 8), (1, n)], 0, SC)).then_inc(t_ready, 16)
                elif kind == "y5":
                    b, par = s[1:]
                    if b:
                        act.wait_ge(y_out, 16 * LC * b)
                    evac(s, V(YP + par * NC5, [(2 * NC5, 4), (1, NC5)]), ([(NC5, 4), (1, NC5)],))
                    if par:
                        for x in range(2):
                            see_copy(act, ("y5", b, x))
                        for j in range(LC):
                            act.dma_start(DV(y_d, b * P * S + j * NC5, [(S, SC), (SC * S, 8), (1, NC5)]),
                                          V(YP, [(NC5, 8), (1, NC5)], SC * j, SC)).then_inc(y_out, 16)
                elif kind == "hk":
                    h = s[1]
                    if h >= 2:
                        see_bank(act, ("hu", h - 2))
                    evac(s, F(HKN + (h % 2) * 384, 384), ([(1, 384)],))
                elif kind == "ho":
                    h = s[1]
                    bank = see_bank(act, s)
                    if h:
                        act.wait_ge(ho_ready, h)
                    deviation([B(bank, [(1, P)], off=t * P) for t in range(TB)], F(HSQ, P), SM + 16, HST,
                              HD).then_inc(ho_std, 1)
                elif kind == "ao" and s[2] == TB - 1:
                    h = s[1]
                    act.wait_ge(full[7], h + 1)
                    act.wait_ge(w_ready, TB * (h + 1))
                    if h:
                        act.wait_ge(ao_ready, h)
                    deviation([B(7, [(1, P)], off=t * P) for t in range(TB)], F(ASQ, P), SM + 20, HST + TB, AV,
                              R0 + (h % 2) * TB).then_inc(ao_std, 1)
                elif kind == "hz":
                    evac(s, F(M0 + (11 + s[1]) * S, S), ([(1, S)],), scale=F(HNG, 1))
                elif kind == "al" and s[3] == 1:
                    u = s[1] * TB + s[2]
                    n = (s[2] + 1) * P
                    act.wait_ge(l_ready, u + 1)
                    for m in range(2):
                        x = F(AL[u % 2] + m * 512, n)
                        last = A(x, x, ACT.Exp, bias=F(SM + (u % 2) * 8 + m, 1), accum_out=F(SM + (u % 2) * 8 + 2 + m, 1))
                    last.then_inc(e_ready, 1)
                elif kind == "aw":
                    u = s[1] * TB + s[2]
                    n = (s[2] + 1) * P
                    evac(s, F(AWT[u % 2], n), ([(1, n)],))
                elif kind == "az":
                    if s[1] == 0:
                        act.wait_ge(s5_mixed, NB5)
                    evac(s, F(M0 + s[1] * S, S), ([(1, S)],), scale=F(SUBG, 1))
                elif kind == "hT":
                    t, q = s[1:]
                    evac(s, V(M0 + 4 * q * S + t * P, [(S, 4), (1, P)]), ([(P, 4), (1, P)],))

            def gelu(b):
                act.wait_ge(yT_sum, b + 1)
                A(F(ZT + b * S, S), F(YT, S), ACT.Gelu_apprx_tanh).then_inc(z_ready, 1)

            for s in steps:
                if s == ("hT", 0, 0):
                    act.wait_ge(squares_sum, 1)
                    A(F(STD, TB), F(SSQ, TB), ACT.Sqrt, scale=1.0 / D, bias=F(EPSC, 1)).then_inc(h_std, 1)
                do(s)
                if s[0] == "pj" and s[1:] in GELU_AFTER:
                    gelu(GELU_AFTER[s[1:]])
                if s == ("pj", "gh", HH - 1):
                    gelu(NB5 - 1)
            act.wait_ge(groups_diff, 1)
            A(F(RGE, 16), F(RGD, 16), ACT.Exp).then_inc(groups_exp, 1)
            act.wait_ge(gates_diff, 1)
            A(F(RE2, TB), F(RDF, TB), ACT.Exp).then_inc(gates_exp, 1)

            def tile(n, parts):
                slot, before = parts[1]
                act.wait_ge(slot_used[slot], before + 2)
                act.wait_ge(h_done, n + 1)
                A(F(SIL, 4 * CAP), B(2, [(1, 4 * CAP)]), ACT.Silu).then_inc(silu_done, 1)
                for q in (0, 2):
                    act.wait_ge(y_full, 3 * n + q + 1)
                    act.wait_ge(ysb_free, n + 1)
                    A(F(YSB + q * 512, 512, 0, CAP), B(4 + q, [(1, 512)], 0, CAP), ACT.Copy).then_inc(y_act, 1)

            with act.Fori(0, NE // 4) as it:
                for k in range(4):
                    tile(it * 4 + k, [main_part(it, k, j) for j in range(6)])
            act.wait_ge(slots_ready, 1)
            flag = act.value_load(F(EID + NOV, 1, 0, 1).bitcast(I32), min_val=0, max_val=NOV)
            with act.If(flag > 0):
                with act.Fori(0, NOV // 2) as it:
                    for k in range(2):
                        tile(it * 2 + k + NE, [over_part(it, k, j) for j in range(6)])
            for t in range(TB):
                act.wait_ge(sum_ready, t + 1)
                deviation([F(H0 + t * D, D)], F(A0 + D * (2 + 2 * t), D), SSQ + t, STD + t, D).then_inc(sum_std, 1)

        @block.vector
        def _(dve):
            v = nc.vector
            n_step = [0]

            def put(ins):
                n_step[0] += 1
                ins.then_inc(dve_step, 1)

            def settle(ins=None):
                if ins is not None:
                    put(ins)
                dve.wait_ge(dve_step, n_step[0])

            def tt(o, a, b, op):
                return v.tensor_tensor(o, a, b, op)

            def ts(o, a, s1, s2, op0, op1=None):
                return v.tensor_scalar(o, a, s1, s2, op0, op1) if op1 is not None else v.tensor_scalar(o, a, s1, None, op0)

            M, AD, SU = ALU.mult, ALU.add, ALU.subtract
            v.memset(F(EPSC, 1), EPS).then_inc(eps_set, 1)
            def R(i):
                return F(DS + i * P, P, 0, NQ)

            def disc_a():
                dve.wait_ge(disc_in, 48)
                settle(ts(R(0), R(0), -1e-4, None, ALU.min))
                dve.wait_ge(disc_act, 1)
                put(tt(R(4), R(1), R(2), M))
                tt(R(3), R(0), R(2), M).then_inc(disc_dve, 1)
                settle()
                settle(ts(R(5), R(4), 1.0 / (2 * math.pi), 12582912.0, M, AD))
                settle(ts(R(5), R(5), 12582912.0, None, SU))
                settle(v.scalar_tensor_tensor(R(6), R(5), -6.28125, R(4), M, AD))
                settle(v.scalar_tensor_tensor(R(6), R(5), -(2 * math.pi - 6.28125), R(6), M, AD))
                ts(R(6), R(6), 3.1415925, -3.1415925, ALU.min, ALU.max).then_inc(disc_dve, 1)
                dve.wait_ge(params_in, 16 * 12)
                tt(F(LB, HH), F(LBL, HH), F(LBL, HH), SU).then_inc(lb_dve, 1)
                tt(V(LAMP, [(SN, 2), (1, SN)]), V(LAML, [(128, 2), (1, SN)]), V(LAML + SN, [(128, 2), (1, SN)]),
                   M).then_inc(dve_step, 1)
                n_step[0] += 1
                settle()
                v.tensor_reduce(F(LAMD, 2), V(LAMP, [(SN, 2), (1, SN)]), AX.X, AD).then_inc(lam_dve, 1)
                settle(ts(F(SUBG, 1), F(SUB, 1), 1.0 - LAM_INIT, None, M))

            def disc_b():
                dve.wait_ge(disc_act, 3)
                settle(tt(R(9), R(8), R(8), M))
                settle(ts(R(9), R(9), -2.0, 1.0, M, AD))
                put(tt(R(10), R(3), R(9), M))
                settle(tt(R(11), R(3), R(7), M))
                put(ts(R(12), R(10), 1.0, None, SU))
                put(tt(R(5), R(0), R(0), M))
                settle(tt(R(6), R(1), R(1), M))
                settle(tt(R(13), R(5), R(6), AD))
                put(v.reciprocal(R(13), R(13)))
                put(tt(R(5), R(12), R(0), M))
                put(tt(R(6), R(11), R(1), M))
                put(tt(R(7), R(11), R(0), M))
                settle(tt(R(8), R(12), R(1), M))
                put(tt(R(5), R(5), R(6), AD))
                settle(tt(R(7), R(7), R(8), SU))
                put(tt(R(14), R(5), R(13), M))
                tt(R(15), R(7), R(13), M).then_inc(disc_done, 1)
                settle()
                dve.wait_ge(lb_act, 1)
                settle(v.reciprocal(F(LBR, HH), F(LBE, HH)))
                settle(tt(F(LBE, HH), F(LBE, HH), F(LBR, HH), M))
                settle(tt(F(LB, HH), F(LBE, HH), F(LBE, HH), SU))
                settle(ts(F(LB1, HH), F(LB, HH), -1.0, 1.0, M, AD))
                dve.wait_ge(lam_act, 1)
                settle(ts(F(NLAM, 1), F(LAME + 1, 1), -LAM_INIT, None, AD))
                settle(tt(F(NLAM, 1), F(NLAM, 1), F(LAME, 1), SU))
                v.nop().then_inc(lam_dve, 1)

            def cmul(o, a, b, dims_o, dims_a, dims_b, n):
                t = [F(ST + 256 * i, n) for i in range(4)]

                def shaped(x, dims):
                    st = 1
                    out_ = []
                    for _, c in reversed(dims):
                        out_.append((st, c))
                        st *= c
                    return V(x, list(reversed(out_)))

                for i, (x, y) in enumerate(((0, 0), (1, 1), (0, 1), (1, 0))):
                    put(tt(shaped(ST + 256 * i, dims_a), V(a[x], dims_a), V(b[y], dims_b), M))
                settle()
                put(tt(V(o[0], dims_o), shaped(ST, dims_a), shaped(ST + 256, dims_a), SU))
                settle(tt(V(o[1], dims_o), shaped(ST + 512, dims_a), shaped(ST + 768, dims_a), AD))

            def tables():
                bank = see_bank(dve, ("ab",))
                put(v.tensor_copy(F(PW + NQ, NQ), B(bank, [(1, NQ)])))
                put(v.tensor_copy(F(PW + 180 + NQ, NQ), B(bank, [(1, NQ)], off=NQ)))
                v.tensor_copy(F(FRI, 2 * NQ), B(bank, [(1, 2 * NQ)], off=2 * NQ)).then_inc(free[bank], 1)
                dve.wait_ge(free[bank], use[("ab",)][1] + 1)
                put(v.memset(F(PW, NQ), 1.0))
                put(v.memset(F(PW + 180, NQ), 0.0))
                settle()
                p = (PW, PW + 180)
                for n in (1, 2, 4):
                    cmul([x + (n + 1) * NQ for x in p], [x + NQ for x in p], [x + n * NQ for x in p],
                         [(NQ, n), (1, NQ)], [(NQ, n), (1, NQ)], [(0, n), (1, NQ)], n * NQ)
                settle(ts(F(PW + 360, 180), F(PW + 180, 180), -1.0, None, M))
                for x in range(2):
                    for j in range(LC):
                        put(v.tensor_copy(F(PR + x * 160 + j * NQ, NQ), F(PW + x * 180 + (7 - j) * NQ, NQ)))
                    put(v.tensor_copy(F(SP + x * 120, NQ), F(PW + x * 180 + 8 * NQ, NQ)))
                settle()
                for l in range(1, 6):
                    a = [SP + x * 120 + (l - 1) * NQ for x in range(2)]
                    cmul([x + NQ for x in a], a, a, [(1, NQ)], [(1, NQ)], [(1, NQ)], NQ)
                for q0 in (0, 10):
                    cmul([BB + x * 320 + q0 * SC for x in range(2)], [BRAW + x * 320 + q0 * SC for x in range(2)],
                         [FRI + x * NQ + q0 for x in range(2)],
                         [(SC, 10), (1, SC)], [(SC, 10), (1, SC)], [(1, 10), (0, SC)], 160)
                for i in range(3):
                    s = ("cT", i)
                    bank = see_bank(dve, s)
                    tiles = [(i, 0, 4, 0)] if i < 2 else [(0, 4, 1, 0), (1, 4, 1, P)]
                    for ri, t0, nt, off in tiles:
                        for par in range(2):
                            for t in range(nt):
                                last = v.tensor_copy(
                                    V(CRI + ri * 320 + (t0 + t) * 4 * SC, [(SC, 4), (1, SC)], par * SN, SN),
                                    B(bank, [(2 * SC, 4), (1, SC)], par * SN, SN, off=off + t * P + par * SC))
                                if not (ri == tiles[-1][0] and par == 1 and t == nt - 1):
                                    put(last)
                    last.then_inc(free[bank], 1)
                    dve.wait_ge(free[bank], use[s][1] + 1)
                settle()
                v.nop().then_inc(tables_ready, 1)
                for i in range(2):
                    s = ("rb", i)
                    bank = see_bank(dve, s)
                    tt(F(RR + i * 320, 320, 0, AH), B(bank, [(1, 320)], 0, AH), F(RM + i * 320, 320, 0, AH),
                       AD).then_inc(free[bank], 1)
                    dve.wait_ge(free[bank], use[s][1] + 1)
                v.nop().then_inc(bias_row, 1)

            def scan(b):
                s = ("st", b)
                bank = see_bank(dve, s)
                if b:
                    see_bank(dve, ("y5", b - 1, 1))
                v.tensor_copy(F(SX, 512), B(bank, [(1, 512)])).then_inc(free[bank], 1)
                dve.wait_ge(free[bank], use[s][1] + 1)
                for l in range(6):
                    sh = 1 << l
                    n = NC5 - sh
                    x = [V(SX + r * 256, [(NC5, QB), (1, n)]) for r in range(2)]
                    a = [V(SP + r * 120 + l * NQ + QB * b, [(1, QB), (0, n)]) for r in range(2)]
                    t = [V(ST + 256 * i, [(NC5, QB), (1, n)]) for i in range(4)]
                    for i, (p, q) in enumerate(((0, 0), (1, 1), (0, 1), (1, 0))):
                        put(tt(t[i], a[p], x[q], M))
                    settle()
                    put(tt(t[0], t[0], t[1], SU))
                    settle(tt(t[2], t[2], t[3], AD))
                    y = [V(SX + r * 256 + sh, [(NC5, QB), (1, n)]) for r in range(2)]
                    put(tt(y[0], y[0], t[0], AD))
                    settle(tt(y[1], y[1], t[2], AD))
                v.nop().then_inc(scanned, 1)

            def skip(b):
                dve.wait_ge(yT_in, 16 * (b + 1))
                v.scalar_tensor_tensor(F(YT, S), F(UT + b * S, S), F(D5 + b, 1), F(YT, S), M, AD).then_inc(yT_sum, 1)

            def hgrn_prepare():
                for k in ("fh", "qh", "gh"):
                    for j in range(HH):
                        see_copy(dve, ("pj", k, j))
                for h in range(HH):
                    put(ts(F(FT + h * S, S), F(FT + h * S, S), F(LB1 + h, 1), F(LB + h, 1), M, AD))
                    put(ts(F(KT + h * S, S), F(KT + h * S, S), F(LB1 + h, 1), None, M))
                settle(ts(F(QT, HH * S), F(QT, HH * S), HD ** -0.5, None, M))
                v.nop().then_inc(level_ready, 1)

            def level(l):
                if l == 0:
                    dve.wait_ge(s5_mixed, NB5)
                for h in range(HH):
                    s = ("hs", l, h)
                    bank = see_bank(dve, s)
                    o = V(HAT + h * S, [(P, TB), (1, P)])
                    x = B(bank, [(P, TB), (1, P)])
                    if l == 0:
                        tt(o, x, V(IDENT, [(0, TB), (1, P)]), M).then_inc(free[bank], 1)
                    else:
                        v.copy_predicated(o, V(C[f"mask{LEVELS[l - 1]}"], [(0, TB), (1, P)]).bitcast(U32),
                                          x).then_inc(free[bank], 1)
                dve.wait_ge(free[bank], use[s][1] + 1)
                if l == 0:
                    settle(tt(F(QT, HH * S), F(QT, HH * S), F(FT, HH * S), M))
                else:
                    L = LEVELS[l - 1]
                    n2 = HH * S // (2 * L)
                    src = FT if l % 2 == 1 else HT2
                    dst = TOT if l == 7 else (HT2 if l % 2 == 1 else FT)
                    put(tt(V(QT + L, [(2 * L, n2), (1, L)]), V(QT + L, [(2 * L, n2), (1, L)]),
                           V(src, [(2, n2), (0, L)]), M))
                    put(tt(V(KT, [(2 * L, n2), (1, L)]), V(KT, [(2 * L, n2), (1, L)]),
                           V(src + 1, [(2, n2), (0, L)]), M))
                    settle(tt(F(dst, n2), V(src, [(2, n2)]), V(src + 1, [(2, n2)]), M))
                v.nop().then_inc(level_ready, 1)

            def hgrn_states(h):
                s = ("hu", h)
                bank = see_bank(dve, s)
                x = [F(HS + (h * 3 + t) * P, P) for t in range(3)]
                settle(v.tensor_copy(x[0], B(bank, [(1, P)])))
                settle(v.scalar_tensor_tensor(x[1], x[0], F(TOT + h * TB + 1, 1), B(bank, [(1, P)], off=P), M, AD))
                v.scalar_tensor_tensor(x[2], x[1], F(TOT + h * TB + 2, 1), B(bank, [(1, P)], off=2 * P), M,
                                       AD).then_inc(free[bank], 1)

            def hgrn_out(h):
                s = ("ho", h)
                bank = see_bank(dve, s)
                dve.wait_ge(ho_std, h + 1)
                settle(v.reciprocal(F(HST, TB), F(HST, TB)))
                tt(V(HO, [(P, TB), (1, P)]), B(bank, [(P, TB), (1, P)]), V(HST, [(1, TB), (0, P)]),
                   M).then_inc(free[bank], 1)
                dve.wait_ge(free[bank], use[s][1] + 1)
                gate = V(GH + h * P, [(640, TB), (1, P)])
                tt(gate, gate, V(HO, [(P, TB), (1, P)]), M).then_inc(ho_ready, 1)
                dve.wait_ge(ho_ready, h + 1)

            def logits(u):
                h, i = units[u]
                n = (i + 1) * P
                if i == 0:
                    dve.wait_ge(strip_in[h % 2], 16 * (h // 2 + 1))
                for m in range(2):
                    s = ("al", h, i, m)
                    bank = see_bank(dve, s)
                    v.scalar_tensor_tensor(F(AL[u % 2] + m * 512, n), B(bank, [(1, n)]), QK ** -0.5,
                                           F(STRIP + (h % 2) * 512 + 512 - n, n), M, AD).then_inc(free[bank], 1)
                for m in range(2):
                    bank, c = use[("al", h, i, m)]
                    dve.wait_ge(free[bank], c + 1)
                if i == TB - 1:
                    v.nop().then_inc(strip_used, 1)
                sm = SM + (u % 2) * 8
                settle(v.tensor_reduce(F(sm, 2), V(AL[u % 2], [(512, 2), (1, n)]), AX.X, ALU.max))
                ts(F(sm, 2), F(sm, 2), -1.0, None, M).then_inc(l_ready, 1)

            def weights(u):
                h, i = units[u]
                n = (i + 1) * P
                sm = SM + (u % 2) * 8
                dve.wait_ge(e_ready, u + 1)
                put(v.reciprocal(F(R0 + (h % 2) * TB + i, 1), F(sm + 2, 1)))
                settle(v.reciprocal(F(sm + 4, 1), F(sm + 3, 1)))
                settle(ts(F(sm + 4, 1), F(sm + 4, 1), F(sm + 2, 1), F(NLAM, 1), M, M))
                if u >= 2:
                    see_bank(dve, ("aw",) + units[u - 2])
                v.scalar_tensor_tensor(F(AW[u % 2], n), F(AL[u % 2] + 512, n), F(sm + 4, 1), F(AL[u % 2], n), M,
                                       AD).then_inc(w_ready, 1)
                dve.wait_ge(w_ready, u + 1)

            def attn_out(h):
                s = ("ao", h, TB - 1)
                bank = 7
                dve.wait_ge(full[7], h + 1)
                if h:
                    see_bank(dve, ("az", h - 1))
                dve.wait_ge(ao_std, h + 1)
                settle(v.reciprocal(F(HST + TB, TB), F(HST + TB, TB)))
                settle(tt(F(HST + TB, TB), F(HST + TB, TB), F(R0 + (h % 2) * TB, TB), M))
                tt(V(AO, [(P, TB), (1, P)]), B(bank, [(P, TB), (1, P)]), V(HST + TB, [(1, TB), (0, P)]),
                   M).then_inc(free[7], 1)
                dve.wait_ge(free[7], h + 1)
                v.nop().then_inc(ao_ready, 1)

            def do(s):
                kind = s[0]
                if kind == "xT":
                    t, q = s[1:]
                    for t1 in [0] * ((t, q) == (0, 0)) + [t + 1] * (q == 1 and t + 1 < TB):
                        dve.wait_ge(x_std, t1 + 1)
                        settle(v.reciprocal(F(RST + t1, 1), F(STD + t1, 1)))
                        if t1 == 0:
                            dve.wait_ge(consts_in, 32)
                        ts(F(DIAG + t1 * P, P), F(IDENT, P), F(RST + t1, 1), None, M).then_inc(x_diag, 1)
                    bank = see_bank(dve, s)
                    tt(V(X0 + 4 * q * S + t * P, [(S, 4), (1, P)]), B(bank, [(P, 4), (1, P)]),
                       V(GMIX + 4 * q, [(1, 4), (0, P)]), M).then_inc(free[bank], 1)
                    if (t, q) == (3, 3):
                        disc_a()
                        disc_b()
                elif kind == "rb" and s[1] == 1:
                    tables()
                elif kind == "st":
                    scan(s[1])
                elif kind == "pj" and s[1:] in GELU_AFTER:
                    skip(GELU_AFTER[s[1:]])
                elif s == ("pj", "gh", HH - 1):
                    skip(NB5 - 1)
                    hgrn_prepare()
                elif kind == "pj" and s[1] == "glu":
                    j = s[2]
                    see_copy(dve, s)
                    tt(V(MS5 + j * S, [(1, LC), (LC, NC5)]), V(ST + (j % 2) * S, [(NC5, LC), (1, NC5)]),
                       V(ZT + j * S, [(NC5, LC), (1, NC5)]), M).then_inc(s5_mixed, 1)
                elif kind == "hs" and s[2] == HH - 1:
                    level(s[1])
                elif kind == "hu":
                    hgrn_states(s[1])
                elif kind == "ho":
                    hgrn_out(s[1])
                elif kind == "al" and s[3] == 1:
                    u = s[1] * TB + s[2]
                    if u == 0:
                        see_bank(dve, ("hz", HH - 1))
                    logits(u)
                    if u >= 1:
                        weights(u - 1)
                    if u >= 6 and u % TB == 2:
                        attn_out(u // TB - 1)
                elif s == ("az", AH - 1):
                    weights(len(units) - 1)
                    attn_out(AH - 1)
                elif kind == "pj" and s[1] == "wo":
                    j = s[2]
                    if j == 0:
                        dve.wait_ge(x_again, 16 * TB)
                    bank = see_bank(dve, s)
                    o = V(H0 + j * P, [(D, TB), (1, P)])
                    tt(o, B(bank, [(P, TB), (1, P)]), o, AD).then_inc(free[bank], 1)
                elif kind == "hT" and s[2] == 0:
                    t = s[1]
                    if t == 0:
                        dve.wait_ge(squares_done, 16 * TB)
                        v.tensor_reduce(F(SSQ, TB), V(SSP, [(16, TB), (1, 16)]), AX.X, AD).then_inc(squares_sum, 1)
                        dve.wait_ge(gf_in, 16)
                        dve.wait_ge(h_std, 1)
                        settle(v.reciprocal(F(RST, TB), F(STD, TB)))
                    if t >= 2:
                        dve.wait_ge(hs_out[t % 2], 16)
                        for q in range(4):
                            see_bank(dve, ("hT", t - 2, q))
                    v.scalar_tensor_tensor(F(HSB[t % 2], D), F(H0 + t * D, D), F(RST + t, 1), F(GF, D), M,
                                           M).then_inc(hs_ready, 1)

            for s in steps:
                do(s)

            s = ("rt",)
            bank = see_bank(dve, s)
            v.tensor_copy(F(RLT, S, 0, 36), B(bank, [(1, S)], 0, 36)).then_inc(free[bank], 1)
            s = ("rT",)
            bank = see_bank(dve, s)
            v.tensor_copy(F(RLG, 144), B(bank, [(1, 144)])).then_inc(free[bank], 1)
            dve.wait_ge(free[bank], use[s][1] + 1)
            put(v.memset(F(RPX, NE), 0.0))
            for k in range(2):
                put(ts(F(IDS + k * TB, TB), F(C["tok"], TB), float(k * S + 1), None, AD))
            gl, el = V(RLG, [(36, TB), (1, NGRP)]), V(RLG + 4, [(36, TB), (1, NE)])

            def first_max(x, n, mx, oh, tmp, cm):
                settle(v.tensor_reduce(F(mx, TB), x, AX.X, ALU.max))
                settle(tt(V(tmp, [(n, TB), (1, n)]), x, V(mx, [(1, TB), (0, n)]), ALU.is_equal))
                settle(tt(V(tmp, [(n, TB), (1, n)]), V(tmp, [(n, TB), (1, n)]), V(C["rev"], [(0, TB), (1, n)]), M))
                settle(v.tensor_reduce(F(cm, TB), V(tmp, [(n, TB), (1, n)]), AX.X, ALU.max))
                settle(tt(V(oh, [(n, TB), (1, n)]), V(tmp, [(n, TB), (1, n)]), V(cm, [(1, TB), (0, n)]), ALU.is_equal))

            first_max(gl, NGRP, RGM, ROG, RTMP, RCM)
            tt(V(RGD, [(4, TB), (1, 4)]), gl, V(RGM, [(1, TB), (0, 4)]), SU).then_inc(groups_diff, 1)
            settle(ts(F(ROG, 16), F(ROG, 16), 1.0, BIG, SU, M))
            settle(tt(V(REL, [(NE, TB), (EPG, NGRP), (1, EPG)]), V(RLG + 4, [(36, TB), (EPG, NGRP), (1, EPG)]),
                      V(ROG, [(4, TB), (1, NGRP), (0, EPG)]), AD))
            ex = V(REL, [(NE, TB), (1, NE)])
            first_max(ex, NE, RV1, RO1, RTMP, RCM)
            settle(v.scalar_tensor_tensor(F(REL, 128), F(RO1, 128), -BIG, F(REL, 128), M, AD))
            first_max(ex, NE, RV2, RO2, RTMP, RCM)
            tt(F(RDF, TB), F(RV2, TB), F(RV1, TB), SU).then_inc(gates_diff, 1)
            settle(tt(F(AS, 128), F(RO1, 128), F(RO2, 128), AD))
            v.nop().then_inc(onehots_ready, 1)
            dve.wait_ge(groups_exp, 1)
            settle(v.tensor_reduce(F(RGS, TB), V(RGE, [(4, TB), (1, 4)]), AX.X, AD))
            put(v.reciprocal(F(RGS, TB), F(RGS, TB)))
            dve.wait_ge(gates_exp, 1)
            settle(ts(F(RDF, TB), F(RE2, TB), 1.0, None, AD))
            settle(v.reciprocal(F(RDF, TB), F(RDF, TB)))
            settle(tt(F(GATE, TB), F(RGS, TB), F(RDF, TB), M))
            settle(tt(F(GATE + TB, TB), F(GATE, TB), F(RE2, TB), M))
            s = ("rk",)
            bank = see_bank(dve, s)
            for t in range(TB):
                settle(tt(F(RPX + (t + 1) * NE, NE), F(RPX + t * NE, NE), B(bank, [(1, NE)], off=(TB + t) * NE), AD))
            tt(F(RKS, TB * NE), F(RPX, TB * NE), B(bank, [(1, TB * NE)]), AD).then_inc(free[bank], 1)
            dve.wait_ge(free[bank], use[s][1] + 1)
            RCN = RPX + TB * NE
            nj = (S - 1) // CAP
            more = V(RBG, [(nj, NE), (1, nj)])
            assert nj <= NOV
            settle(tt(more, V(RCN, [(1, NE), (0, nj)]), V(C["base"] + 1, [(0, NE), (1, nj)]), ALU.is_gt))
            settle(v.tensor_reduce(F(RNV, NE), more, AX.X, AD))
            settle(v.tensor_tensor_scan(F(RCU, NE), F(C["ones"], NE), F(RNV, NE), 0.0, M, AD))
            settle(tt(F(ROB, NE), F(RCU, NE), F(RNV, NE), SU))
            settle(v.scalar_tensor_tensor(F(ROB, NE), F(ROB, NE), float(CAP), F(C["over"], NE), M, AD))
            rk = V(RKS, [(NE, TB), (1, NE)])
            all3 = [(NE, TB), (1, NE)]
            settle(ts(V(RTMP, all3), rk, float(CAP), None, ALU.is_ge))
            settle(tt(V(RTMP, all3), V(RTMP, all3), V(ROB, [(0, TB), (1, NE)]), M))
            settle(tt(V(REL, all3), rk, V(C["base"], [(0, TB), (1, NE)]), AD))
            settle(tt(F(REL, 128), F(REL, 128), F(RTMP, 128), AD))
            for k, oh in enumerate((RO1, RO2)):
                settle(tt(F(RTMP, 128), F(oh, 128), F(REL, 128), M))
                settle(v.tensor_reduce(F(RPF + k * TB, TB), V(RTMP, all3), AX.X, AD))
            for t in (2, 3):
                for q in range(4):
                    see_bank(dve, ("hT", t, q))
                dve.wait_ge(hs_out[t % 2], 32)
            ge = V(RGE_T, [(NT + 1, NAS), (1, NT + 1)])
            at_tile = V(ROT, [(NT, NAS), (1, NT)])
            settle(tt(ge, V(RPF, [(1, NAS), (0, NT + 1)]), V(C["base"], [(0, NAS), (1, NT + 1)]), ALU.is_ge))
            put(v.tensor_reduce(F(RTL, NAS), ge, AX.X, AD))
            settle(tt(at_tile, V(RGE_T, [(NT + 1, NAS), (1, NT)]), V(RGE_T + 1, [(NT + 1, NAS), (1, NT)]), SU))
            put(tt(at_tile, at_tile, V(IDS, [(1, NAS), (0, NT)]), M))
            settle(v.scalar_tensor_tensor(F(RSL, NAS), F(RTL, NAS), -float(CAP), F(RPF, NAS), M, AD))
            settle(tt(V(ROS, [(CAP, NAS), (1, CAP)]), V(RSL, [(1, NAS), (0, CAP)]), V(C["slot"], [(0, NAS), (1, CAP)]),
                      ALU.is_equal))
            v.nop().then_inc(places_ready, 1)
            settle(tt(V(RBG, [(NE, NOV), (1, NE)]), V(RCU, [(0, NOV), (1, NE)]), V(C["ovi"], [(1, NOV), (0, NE)]),
                      ALU.is_le))
            settle(v.tensor_reduce(F(REI, NOV), V(RBG, [(NE, NOV), (1, NE)]), AX.X, AD))
            settle(ts(F(REI, NOV), F(REI, NOV), float(NE - 1), None, ALU.min))
            settle(v.tensor_copy(F(REI + NOV, 1), F(RCU + NE - 1, 1)))
            settle(v.tensor_copy(F(EID, NOV + 1).bitcast(I32), F(REI, NOV + 1)))
            settle(v.memset(F(SLOTF, NT + 2), SENT))
            s = ("id",)
            bank = see_bank(dve, s)
            got = B(bank, [(1, NT)], 0, CAP)
            settle(ts(F(TOKU, NT, 0, CAP), got, 0.0, SENT + 1, ALU.is_equal, M))
            v.scalar_tensor_tensor(F(SLOTF, NT, 0, CAP), got, -1.0, F(TOKU, NT, 0, CAP), AD, AD).then_inc(free[bank], 1)
            dve.wait_ge(free[bank], use[s][1] + 1)
            settle(v.tensor_copy(F(DSTU, NT + 2).bitcast(U32), F(SLOTF, NT + 2)))
            settle(ts(F(TOKU, NT + 2), F(SLOTF, NT + 2), float(S), -float(S), ALU.is_ge, M))
            settle(tt(F(SLOTF, NT + 2), F(SLOTF, NT + 2), F(TOKU, NT + 2), AD))
            settle(v.tensor_copy(F(TOKU, NT + 2).bitcast(U32), F(SLOTF, NT + 2)))
            v.nop().then_inc(slots_ready, 1)

            def turned(n):
                for f in range(4):
                    dve.wait_ge(xT_full, 4 * n + f + 1)
                    v.tensor_copy(F(XT + 4 * f * CAP, 4 * CAP), B(TURN_BANK[f], [(1, 4 * CAP)])).then_inc(xT_free, 1)

            def tile(n, parts):
                slot, before = parts[3]
                dve.wait_ge(slot_used[slot], before + 2)
                dve.wait_ge(silu_done, n + 2)
                tt(F(HTE, 4 * CAP), F(SIL, 4 * CAP), B(3, [(1, 4 * CAP)]), M).then_inc(h_done, 1)
                turned(n + 1)
                dve.wait_ge(y_full, 3 * n + 2)
                dve.wait_ge(ysb_free, n + 1)
                v.tensor_copy(F(YSB + 512, 512, 0, CAP), B(5, [(1, 512)], 0, CAP)).then_inc(y_dve, 1)
                slot, before = parts[5]
                dve.wait_ge(slot_used[slot], before + 2)
                v.tensor_copy(F(YSB + 3 * 512, 512, 0, CAP), B(7, [(1, 512)], 0, CAP)).then_inc(y_dve, 1)

            turned(0)
            with dve.Fori(0, NE // 4) as it:
                for k in range(4):
                    tile(it * 4 + k, [main_part(it, k, j) for j in range(6)])
            flag = dve.value_load(F(EID + NOV, 1, 0, 1).bitcast(I32), min_val=0, max_val=NOV)
            with dve.If(flag > 0):
                with dve.Fori(0, NOV // 2) as it:
                    for k in range(2):
                        tile(it * 2 + k + NE, [over_part(it, k, j) for j in range(6)])

            def total(t):
                dve.wait_ge(fin_in[t], 32)
                x = F(H0 + t * D, D)
                settle(v.scalar_tensor_tensor(x, F(A0 + D * (1 + 2 * t), D), F(GATE + t, 1), x, M, AD))
                v.scalar_tensor_tensor(x, F(A0 + D * (2 + 2 * t), D), F(GATE + TB + t, 1), x, M, AD).then_inc(sum_ready, 1)

            total(0)
            for t in range(TB):
                if t + 1 < TB:
                    total(t + 1)
                if t == 0:
                    dve.wait_ge(fg_in, 16)
                dve.wait_ge(sum_std, t + 1)
                settle(v.reciprocal(F(RST + t, 1), F(STD + t, 1)))
                v.scalar_tensor_tensor(F(A0 + D * (1 + 2 * t), D), F(H0 + t * D, D), F(RST + t, 1), F(A0, D), M,
                                       M).then_inc(out_ready, 1)


_IN = ["x", "w_in", "w_out", "mix_norm_g", "ffn_norm_g", "rel_bias", "diff_lambda", "attn_subln_g", "s5_a_re",
       "s5_a_im", "s5_log_dt", "s5_b_re", "s5_b_im", "s5_c_re", "s5_c_im", "s5_d", "s5_w_glu", "hgrn_lb_logits",
       "hgrn_norm_g", "moe_w_group", "moe_w_router", "moe_w_gate", "moe_w_up", "moe_w_down", "final_norm_g"]


def arrays_of(inputs):
    block, cols, onehot, masked = shape_constants()
    arrays = {}
    for name in _IN:
        a = np.ascontiguousarray(inputs[name])
        arrays[name] = a[0] if a.ndim > 1 and a.shape[0] == 1 else a
    arrays.update(consts=block, onehot=onehot, masked=masked)
    return arrays, cols


def kernel(**inputs):
    import concourse.bacc as _bacc
    from concourse.bass_utils import run_bass_kernel_spmd as _run

    arrays, cols = arrays_of(inputs)
    nc = _bacc.Bacc("TRN2", target_bir_lowering=False, num_devices=1)
    d = {k: nc.dram_tensor(f"in_{k}", a.shape, mybir.dt.from_np(a.dtype), kind="ExternalInput").ap()
         for k, a in arrays.items()}
    out = nc.dram_tensor("out_0", (S, D), F32, kind="ExternalOutput").ap()
    build(nc, d, out, cols)
    r = _run(nc, [{f"in_{k}": a for k, a in arrays.items()}], core_ids=[0])
    return r.results[0]["out_0"].reshape(1, S, D)
```
